# Optimizing a Trainium2 kernel written in Bass

```python
import jax, jax.numpy as jnp
from jax import lax
import numpy as np

D_MODEL = 1024
BATCH = 1
SEQ = 256
DEPTH = 2

GRID_W = 64
CTX_LEN = 256
N_EVEN = (DEPTH + 1) // 2
N_ODD = DEPTH // 2

MLA_HEADS = 8
QK_NOPE_DIM = 64
QK_ROPE_DIM = 32
QK_HEAD_DIM = QK_NOPE_DIM + QK_ROPE_DIM
V_HEAD_DIM = 64
Q_LORA_RANK = 384
KV_LORA_RANK = 256
QK_SCALE = QK_HEAD_DIM ** -0.5
ROPE_BASE = 10000.0
BLOCK_Q = 128
CONV_GROUPS = 8
CONV_GROUP_DIM = 64
CONV_DIM = CONV_GROUPS * CONV_GROUP_DIM
CONV_WIDTH = 3
CONV_OFFSET = Q_LORA_RANK + KV_LORA_RANK + QK_ROPE_DIM
IN_PROJ_DIM = CONV_OFFSET + 3 * CONV_DIM
MIX_OUT_DIM = MLA_HEADS * V_HEAD_DIM + CONV_DIM
FOURIER_GROUPS = 4
FOURIER_GROUP_DIM = D_MODEL // FOURIER_GROUPS
D_FF = ((8 * D_MODEL + 3 * 256 - 1) // (3 * 256)) * 256
EPS = 1e-6


def rmsnorm(x, g):
    xf = x.astype(jnp.float32)
    y = xf * lax.rsqrt(jnp.mean(xf * xf, axis=-1, keepdims=True) + EPS)
    return (y * g.astype(jnp.float32)).astype(x.dtype)

def axial_angles(T):
    rows = T // GRID_W
    row = jnp.broadcast_to(jnp.arange(rows)[:, None], (rows, GRID_W)).reshape(-1).astype(jnp.float32)
    col = jnp.broadcast_to(jnp.arange(GRID_W)[None, :], (rows, GRID_W)).reshape(-1).astype(jnp.float32)
    half = QK_ROPE_DIM // 2
    inv = 1.0 / (ROPE_BASE ** (jnp.arange(0, half, 2, dtype=jnp.float32) / half))
    return row[:, None] * inv, col[:, None] * inv

def rotate(x, ang):
    cos = jnp.cos(ang)[:, None, :].astype(x.dtype)
    sin = jnp.sin(ang)[:, None, :].astype(x.dtype)
    x1, x2 = jnp.split(x, 2, axis=-1)
    return jnp.concatenate([x1 * cos - x2 * sin, x2 * cos + x1 * sin], axis=-1)

def axial_rope(x, ang_row, ang_col):
    half = QK_ROPE_DIM // 2
    return jnp.concatenate([rotate(x[..., :half], ang_row), rotate(x[..., half:], ang_col)], axis=-1)

def mla_qkv(proj, q_norm_g, kv_norm_g, w_uq, w_ukv, q_gain, k_gain, angles):
    B, T, _ = proj.shape
    cq = proj[..., :Q_LORA_RANK]
    ckv = proj[..., Q_LORA_RANK:Q_LORA_RANK + KV_LORA_RANK]
    k_pe = proj[..., Q_LORA_RANK + KV_LORA_RANK:CONV_OFFSET]
    q = (rmsnorm(cq, q_norm_g) @ w_uq).reshape(B, T, MLA_HEADS, QK_HEAD_DIM)
    kv = (rmsnorm(ckv, kv_norm_g) @ w_ukv).reshape(B, T, MLA_HEADS, QK_NOPE_DIM + V_HEAD_DIM)
    k_nope, v = kv[..., :QK_NOPE_DIM], kv[..., QK_NOPE_DIM:]
    k = jnp.concatenate([k_nope, jnp.broadcast_to(k_pe[:, :, None, :], (B, T, MLA_HEADS, QK_ROPE_DIM))], axis=-1)
    q = rmsnorm(q, q_gain)
    k = rmsnorm(k, k_gain)
    if angles is not None:
        ang_row, ang_col = angles
        q = jnp.concatenate([q[..., :QK_NOPE_DIM], axial_rope(q[..., QK_NOPE_DIM:], ang_row, ang_col)], axis=-1)
        k = jnp.concatenate([k[..., :QK_NOPE_DIM], axial_rope(k[..., QK_NOPE_DIM:], ang_row, ang_col)], axis=-1)
    return q, k, v

def attend(q, k, v):
    s = jnp.einsum('bqhd,bkhd->bhqk', q, k, preferred_element_type=jnp.float32) * QK_SCALE
    p = jax.nn.softmax(s, axis=-1)
    return jnp.einsum('bhqk,bkhd->bqhd', p.astype(v.dtype), v)

def attend_blocked(q, k, v):
    B, S, H, D = q.shape
    nb = S // BLOCK_Q
    qb = q.reshape(B, nb, BLOCK_Q, H, D).transpose(1, 0, 2, 3, 4)
    ob = lax.map(lambda qi: attend(qi, k, v), qb)
    return ob.transpose(1, 0, 2, 3, 4).reshape(B, S, H * V_HEAD_DIM)

def short_conv(p, conv_w):
    b_gate, c_gate, u = jnp.split(p, 3, axis=-1)
    z = c_gate * u
    T = z.shape[1]
    zp = jnp.pad(z, ((0, 0), (1, 1), (0, 0)))
    y = zp[:, 0:T] * conv_w[0] + zp[:, 1:T + 1] * conv_w[1] + zp[:, 2:T + 2] * conv_w[2]
    return b_gate * y

def even_mixer(h_lat, h_ctx, w_in, q_norm_g, kv_norm_g, w_uq, w_ukv, q_gain, k_gain, conv_w, w_o, with_ctx_out):
    B, S, _ = h_lat.shape
    L = h_ctx.shape[1]
    p_lat = h_lat @ w_in
    p_ctx = h_ctx @ w_in
    q_l, k_l, v_l = mla_qkv(p_lat, q_norm_g, kv_norm_g, w_uq, w_ukv, q_gain, k_gain, axial_angles(S))
    q_c, k_c, v_c = mla_qkv(p_ctx, q_norm_g, kv_norm_g, w_uq, w_ukv, q_gain, k_gain, None)
    k_all = jnp.concatenate([k_l, k_c], axis=1)
    v_all = jnp.concatenate([v_l, v_c], axis=1)
    a_l = attend_blocked(q_l, k_all, v_all)
    s_l = short_conv(p_lat[..., CONV_OFFSET:], conv_w)
    out_l = jnp.concatenate([a_l, s_l], axis=-1) @ w_o
    if not with_ctx_out:
        return out_l, None
    a_c = attend(q_c, k_c, v_c).reshape(B, L, MLA_HEADS * V_HEAD_DIM)
    s_c = short_conv(p_ctx[..., CONV_OFFSET:], conv_w)
    out_c = jnp.concatenate([a_c, s_c], axis=-1) @ w_o
    return out_l, out_c

def fourier_mixer(h, w_f):
    B, T, _ = h.shape
    hg = h.astype(jnp.float32).reshape(B, T, FOURIER_GROUPS, FOURIER_GROUP_DIM)
    f = jnp.fft.fft2(hg, axes=(1, 3), norm="ortho").real
    return f.reshape(B, T, D_MODEL).astype(h.dtype) @ w_f

def swiglu(h, w1, w3, w2):
    return (jax.nn.silu(h @ w1) * (h @ w3)) @ w2

def ada(cvec, w, b):
    return jnp.split(jax.nn.silu(cvec) @ w + b, 6, axis=-1)

def first_inputs(seed: int = 0) -> dict:
    key = jax.random.key(seed)
    ks = jax.random.split(key, 24)
    nrm = jax.random.normal
    f32 = jnp.float32
    D = D_MODEL
    return {
        "x": nrm(ks[0], (BATCH, SEQ, D), f32),
        "c": nrm(ks[1], (BATCH, D), f32),
        "ctx": nrm(ks[2], (BATCH, CTX_LEN, D), f32),
        "c_ctx": nrm(ks[3], (D,), f32),
        "ada_w": nrm(ks[4], (DEPTH, D, 6 * D), f32) * D ** -0.5,
        "ada_b": nrm(ks[5], (DEPTH, 6 * D), f32) * 0.01,
        "norm1_g": 1.0 + 0.02 * nrm(ks[6], (DEPTH, D), f32),
        "norm2_g": 1.0 + 0.02 * nrm(ks[7], (DEPTH, D), f32),
        "w_in": nrm(ks[8], (N_EVEN, D, IN_PROJ_DIM), f32) * D ** -0.5,
        "q_norm_g": 1.0 + 0.02 * nrm(ks[9], (N_EVEN, Q_LORA_RANK), f32),
        "kv_norm_g": 1.0 + 0.02 * nrm(ks[10], (N_EVEN, KV_LORA_RANK), f32),
        "w_uq": nrm(ks[11], (N_EVEN, Q_LORA_RANK, MLA_HEADS * QK_HEAD_DIM), f32) * Q_LORA_RANK ** -0.5,
        "w_ukv": nrm(ks[12], (N_EVEN, KV_LORA_RANK, MLA_HEADS * (QK_NOPE_DIM + V_HEAD_DIM)), f32) * KV_LORA_RANK ** -0.5,
        "q_gain": 1.0 + 0.02 * nrm(ks[13], (N_EVEN, QK_HEAD_DIM), f32),
        "k_gain": 1.0 + 0.02 * nrm(ks[14], (N_EVEN, QK_HEAD_DIM), f32),
        "conv_w": nrm(ks[15], (N_EVEN, CONV_WIDTH, CONV_DIM), f32) * CONV_WIDTH ** -0.5,
        "w_o": nrm(ks[16], (N_EVEN, MIX_OUT_DIM, D), f32) * MIX_OUT_DIM ** -0.5,
        "w_fourier": nrm(ks[17], (N_ODD, D, D), f32) * D ** -0.5,
        "ffn_w1": nrm(ks[18], (DEPTH, D, D_FF), f32) * D ** -0.5,
        "ffn_w3": nrm(ks[19], (DEPTH, D, D_FF), f32) * D ** -0.5,
        "ffn_w2": nrm(ks[20], (DEPTH, D_FF, D), f32) * D_FF ** -0.5,
    }

def first_block(x, c, ctx, c_ctx, ada_w, ada_b, norm1_g, norm2_g, w_in, q_norm_g, kv_norm_g, w_uq, w_ukv,
              q_gain, k_gain, conv_w, w_o, w_fourier, ffn_w1, ffn_w3, ffn_w2):
    for i in range(DEPTH):
        last = i == DEPTH - 1
        j = i // 2
        sh1, sc1, g1, sh2, sc2, g2 = [m[:, None, :] for m in ada(c, ada_w[i], ada_b[i])]
        csh1, csc1, cg1, csh2, csc2, cg2 = ada(c_ctx, ada_w[i], ada_b[i])
        h_l = rmsnorm(x, norm1_g[i]) * (1 + sc1) + sh1
        if i % 2 == 0:
            h_c = rmsnorm(ctx, norm1_g[i]) * (1 + csc1) + csh1
            out_l, out_c = even_mixer(h_l, h_c, w_in[j], q_norm_g[j], kv_norm_g[j], w_uq[j], w_ukv[j],
                                      q_gain[j], k_gain[j], conv_w[j], w_o[j], not last)
        else:
            out_l = fourier_mixer(h_l, w_fourier[j])
            out_c = None
            if not last:
                h_c = rmsnorm(ctx, norm1_g[i]) * (1 + csc1) + csh1
                out_c = fourier_mixer(h_c, w_fourier[j])
        x = x + g1 * out_l
        x = x + g2 * swiglu(rmsnorm(x, norm2_g[i]) * (1 + sc2) + sh2, ffn_w1[i], ffn_w3[i], ffn_w2[i])
        if not last:
            ctx = ctx + cg1 * out_c
            ctx = ctx + cg2 * swiglu(rmsnorm(ctx, norm2_g[i]) * (1 + csc2) + csh2, ffn_w1[i], ffn_w3[i], ffn_w2[i])
    return x


POOL_WINDOWS = (2, 4, 8, 16)
POOL_GROUP = 64
POOL_WIDTH = POOL_GROUP * len(POOL_WINDOWS)
ATTN_HEADS = 4
ATTN_HEAD_DIM = 64
ATTN_WIDTH = ATTN_HEADS * ATTN_HEAD_DIM
IDX_HEADS = 8
IDX_DIM = 64
TOPK_MAX = 256
Q_BLOCK = 128
HGRN_HEADS = 4
HGRN_EXPAND = 128
HGRN_HEAD_V = 128
HGRN_KW = HGRN_HEADS * HGRN_EXPAND
HGRN_VW = HGRN_HEADS * HGRN_HEAD_V
HGRN_CHUNK = 64
KEY_MAX = 1.0 - 1e-6
REL_BUCKETS = 32
REL_MAX_DIST = 128
D_FF_2 = 2816
N_SUB = 3
DN_ALPHA = (2 * DEPTH) ** 0.25
DN_BETA = (8 * DEPTH) ** -0.25
LN_EPS = 1e-5
RMS_EPS = 1e-6

MIX_WIDTH = POOL_WIDTH + ATTN_WIDTH + HGRN_VW
MIX_IN_WIDTHS = (POOL_WIDTH, ATTN_WIDTH, ATTN_WIDTH, ATTN_WIDTH, IDX_HEADS * IDX_DIM, IDX_DIM, IDX_HEADS,
                 HGRN_KW, HGRN_KW, HGRN_VW, HGRN_VW, 3 * D_MODEL)
MIX_IN_WIDTH = sum(MIX_IN_WIDTHS)
MIX_SPLITS = tuple(int(s) for s in np.cumsum(MIX_IN_WIDTHS)[:-1])


def layer_norm(x, g, b):
    x32 = x.astype(jnp.float32)
    mu = jnp.mean(x32, axis=-1, keepdims=True)
    var = jnp.mean(jnp.square(x32 - mu), axis=-1, keepdims=True)
    y = (x32 - mu) * lax.rsqrt(var + LN_EPS)
    return (y * g.astype(jnp.float32) + b.astype(jnp.float32)).astype(x.dtype)

def swiglu_2(h, w_in, w_out):
    gate, up = jnp.split(h @ w_in, 2, axis=-1)
    return (jax.nn.silu(gate) * up) @ w_out

def modulate(h, mod, j):
    return h * (1 + mod[:, j, 1][:, None, :]) + mod[:, j, 0][:, None, :]

def sub_gate(mod, j):
    return 1 + mod[:, j, 2][:, None, :]

def pool_mixer(a, pool_w, pool_scale):
    B, S, _ = a.shape
    a32 = a.astype(jnp.float32)
    P = jnp.pad(jnp.cumsum(a32, axis=1), ((0, 0), (1, 0), (0, 0)))
    pos1 = jnp.arange(1, S + 1)
    means = []
    for g, w in enumerate(POOL_WINDOWS):
        Pg = P[..., g * POOL_GROUP:(g + 1) * POOL_GROUP]
        lead = Pg[:, 1:]
        lag = jnp.concatenate([jnp.zeros_like(Pg[:, :w - 1]), Pg[:, :S + 1 - w]], axis=1)
        cnt = jnp.minimum(pos1, w).astype(jnp.float32)
        means.append((lead - lag) / cnt[None, :, None])
    pooled = jnp.stack(means, axis=2)
    d = (pooled - a32.reshape(B, S, len(POOL_WINDOWS), POOL_GROUP)).astype(a.dtype)
    y = jnp.einsum('bsgc,gcd->bsgd', d, pool_w)
    return y.reshape(B, S, POOL_WIDTH) * pool_scale

def t5_bucket(dist):
    max_exact = REL_BUCKETS // 2
    d32 = jnp.maximum(dist, 1).astype(jnp.float32)
    large = max_exact + (jnp.log(d32 / max_exact) / np.log(REL_MAX_DIST / max_exact)
                         * (REL_BUCKETS - max_exact)).astype(jnp.int32)
    large = jnp.minimum(large, REL_BUCKETS - 1)
    return jnp.where(dist < max_exact, dist, large)

def sparse_attention(q, k, v, q_idx, k_idx, w_idx, rel_bias):
    B, S, H, dh = q.shape
    top_k = min(TOPK_MAX, S // 4)
    n_blocks = S // Q_BLOCK
    scale = dh ** -0.5
    idx_scale = (IDX_DIM ** -0.5) * (IDX_HEADS ** -0.5)
    key_pos = jnp.arange(S)

    def block(i):
        q0 = i * Q_BLOCK
        qb = lax.dynamic_slice_in_dim(q, q0, Q_BLOCK, axis=1)
        qib = lax.dynamic_slice_in_dim(q_idx, q0, Q_BLOCK, axis=1)
        wb = lax.dynamic_slice_in_dim(w_idx, q0, Q_BLOCK, axis=1)
        qpos = q0 + jnp.arange(Q_BLOCK)
        logit_idx = jnp.einsum('bqhd,bsd->bqhs', qib, k_idx)
        score = jnp.einsum('bqh,bqhs->bqs', wb, jax.nn.relu(logit_idx)).astype(jnp.float32) * idx_scale
        causal = key_pos[None, :] <= qpos[:, None]
        score = jnp.where(causal[None], score, -jnp.inf)
        _, sel = lax.top_k(score, top_k)
        k_sel = jax.vmap(lambda kk, ii: kk[ii])(k, sel)
        v_sel = jax.vmap(lambda vv, ii: vv[ii])(v, sel)
        logits = jnp.einsum('bqhd,bqkhd->bhqk', qb, k_sel).astype(jnp.float32) * scale
        dist = qpos[None, :, None] - sel
        bias = rel_bias[t5_bucket(jnp.maximum(dist, 0))].astype(jnp.float32)
        logits = logits + jnp.transpose(bias, (0, 3, 1, 2))
        logits = jnp.where((dist >= 0)[:, None], logits, -jnp.inf)
        p = jax.nn.softmax(logits, axis=-1).astype(v.dtype)
        return jnp.einsum('bhqk,bqkhd->bqhd', p, v_sel)

    out = lax.map(block, jnp.arange(n_blocks))
    return jnp.transpose(out, (1, 0, 2, 3, 4)).reshape(B, S, H * dh)

def hgrn2(q, f_logit, i_val, g_out, lb, norm_g):
    B, S, _ = q.shape
    C = HGRN_CHUNK
    NC = S // C
    z = f_logit.astype(jnp.float32)
    lb = lb.astype(jnp.float32)
    key = (1 - lb) * jax.nn.sigmoid(-z)
    log_f = jnp.log1p(-jnp.minimum(key, KEY_MAX))
    qf = jax.nn.silu(q.astype(jnp.float32))

    def to_chunks(t, d):
        return jnp.transpose(t.reshape(B, NC, C, HGRN_HEADS, d), (1, 0, 3, 2, 4))

    qc = to_chunks(qf, HGRN_EXPAND)
    kc = to_chunks(key, HGRN_EXPAND)
    gc = to_chunks(log_f, HGRN_EXPAND)
    vc = to_chunks(i_val.astype(jnp.float32), HGRN_HEAD_V)
    tri = jnp.tril(jnp.ones((C, C), dtype=bool))

    def step(state, inp):
        qq, kk, vv, gg = inp
        A = jnp.cumsum(gg, axis=2)
        o_inter = jnp.einsum('bhtd,bhdv->bhtv', qq * jnp.exp(A), state)
        diff = A[:, :, :, None, :] - A[:, :, None, :, :]
        decay = jnp.exp(jnp.where(tri[None, None, :, :, None], diff, -jnp.inf))
        scores = jnp.einsum('bhtd,bhsd,bhtsd->bhts', qq, kk, decay)
        o_intra = jnp.einsum('bhts,bhsv->bhtv', scores, vv)
        k_dec = kk * jnp.exp(A[:, :, -1:, :] - A)
        new_state = jnp.exp(A[:, :, -1, :])[..., None] * state + jnp.einsum('bhsd,bhsv->bhdv', k_dec, vv)
        return new_state, o_inter + o_intra

    s0 = jnp.zeros((B, HGRN_HEADS, HGRN_EXPAND, HGRN_HEAD_V), jnp.float32)
    _, o = lax.scan(step, s0, (qc, kc, vc, gc))
    o = jnp.transpose(o, (1, 0, 3, 2, 4)).reshape(B, S, HGRN_HEADS, HGRN_HEAD_V)
    o = o * lax.rsqrt(jnp.mean(jnp.square(o), axis=-1, keepdims=True) + RMS_EPS)
    o = o.reshape(B, S, HGRN_VW).astype(q.dtype)
    return o * norm_g * jax.nn.silu(g_out)

def token_mixer(h, w_in, pool_w, pool_scale, rel_bias, lb, norm_g, w_branch, w_out):
    B, S, _ = h.shape
    proj = h @ w_in
    (a, q, k, v, qi, ki, wi, hq, hf, hi, hg, gates) = jnp.split(proj, MIX_SPLITS, axis=-1)
    y_a = pool_mixer(a, pool_w, pool_scale)
    y_b = sparse_attention(q.reshape(B, S, ATTN_HEADS, ATTN_HEAD_DIM),
                           k.reshape(B, S, ATTN_HEADS, ATTN_HEAD_DIM),
                           v.reshape(B, S, ATTN_HEADS, ATTN_HEAD_DIM),
                           qi.reshape(B, S, IDX_HEADS, IDX_DIM), ki, wi, rel_bias)
    y_c = hgrn2(hq, hf, hi, hg, lb, norm_g)
    g = jax.nn.sigmoid(gates.reshape(B, S, 3, D_MODEL))
    merged = (g[:, :, 0] * (y_a @ w_branch[:POOL_WIDTH])
              + g[:, :, 1] * (y_b @ w_branch[POOL_WIDTH:POOL_WIDTH + ATTN_WIDTH])
              + g[:, :, 2] * (y_c @ w_branch[POOL_WIDTH + ATTN_WIDTH:]))
    return merged @ w_out

def second_inputs(seed: int = 0) -> dict:
    key = jax.random.key(seed)
    ks = jax.random.split(key, 16)
    f32 = jnp.float32

    def n(k, shape):
        return jax.random.normal(k, shape, f32)

    x = n(ks[0], (BATCH, SEQ, D_MODEL))
    c = n(ks[1], (BATCH, D_MODEL))
    w_ada = n(ks[2], (DEPTH, D_MODEL, N_SUB * 3 * D_MODEL)) * (0.3 * D_MODEL ** -0.5)
    b_ada = 0.01 * n(ks[3], (DEPTH, N_SUB * 3 * D_MODEL))
    ln_g = 1.0 + 0.02 * n(ks[4], (DEPTH, N_SUB, D_MODEL))
    ln_b = 0.02 * n(ks[5], (DEPTH, N_SUB, D_MODEL))
    ffn_w_in = n(ks[6], (DEPTH, 2, D_MODEL, 2 * D_FF_2)) * D_MODEL ** -0.5
    ffn_w_out = n(ks[7], (DEPTH, 2, D_FF_2, D_MODEL)) * (DN_BETA * D_FF_2 ** -0.5)
    mix_w_in = n(ks[8], (DEPTH, D_MODEL, MIX_IN_WIDTH)) * D_MODEL ** -0.5
    pool_w = n(ks[9], (DEPTH, len(POOL_WINDOWS), POOL_GROUP, POOL_GROUP)) * POOL_GROUP ** -0.5
    pool_scale = 1.0 + 0.02 * n(ks[10], (DEPTH, POOL_WIDTH))
    rel_bias = 0.5 * n(ks[11], (REL_BUCKETS, ATTN_HEADS))
    hgrn_lb = 1.0 + 0.1 * n(ks[12], (DEPTH, HGRN_KW))
    hgrn_norm_g = 1.0 + 0.02 * n(ks[13], (DEPTH, HGRN_VW))
    row_scale = jnp.concatenate([jnp.full((POOL_WIDTH,), POOL_WIDTH ** -0.5, f32),
                                 jnp.full((ATTN_WIDTH,), ATTN_WIDTH ** -0.5, f32),
                                 jnp.full((HGRN_VW,), HGRN_VW ** -0.5, f32)])
    w_branch = n(ks[14], (DEPTH, MIX_WIDTH, D_MODEL)) * row_scale[None, :, None]
    w_out = n(ks[15], (DEPTH, D_MODEL, D_MODEL)) * (DN_BETA * D_MODEL ** -0.5)
    return {'x': x, 'c': c, 'w_ada': w_ada, 'b_ada': b_ada, 'ln_g': ln_g, 'ln_b': ln_b,
            'ffn_w_in': ffn_w_in, 'ffn_w_out': ffn_w_out, 'mix_w_in': mix_w_in,
            'pool_w': pool_w, 'pool_scale': pool_scale, 'rel_bias': rel_bias,
            'hgrn_lb': hgrn_lb, 'hgrn_norm_g': hgrn_norm_g, 'w_branch': w_branch, 'w_out': w_out}

def second_block(x, c, w_ada, b_ada, ln_g, ln_b, ffn_w_in, ffn_w_out, mix_w_in, pool_w, pool_scale,
              rel_bias, hgrn_lb, hgrn_norm_g, w_branch, w_out):
    B = x.shape[0]
    lb_sm = jax.nn.softmax(hgrn_lb.astype(jnp.float32), axis=0)
    lbs = jnp.cumsum(lb_sm, axis=0) - lb_sm[0:1]
    cond = jax.nn.silu(c)
    for l in range(DEPTH):
        mod = (cond @ w_ada[l] + b_ada[l]).reshape(B, N_SUB, 3, D_MODEL)
        y = swiglu_2(modulate(x, mod, 0), ffn_w_in[l, 0], ffn_w_out[l, 0])
        x = layer_norm(DN_ALPHA * x + 0.5 * sub_gate(mod, 0) * y, ln_g[l, 0], ln_b[l, 0])
        y = token_mixer(modulate(x, mod, 1), mix_w_in[l], pool_w[l], pool_scale[l], rel_bias,
                        lbs[l], hgrn_norm_g[l], w_branch[l], w_out[l])
        x = layer_norm(DN_ALPHA * x + sub_gate(mod, 1) * y, ln_g[l, 1], ln_b[l, 1])
        y = swiglu_2(modulate(x, mod, 2), ffn_w_in[l, 1], ffn_w_out[l, 1])
        x = layer_norm(DN_ALPHA * x + 0.5 * sub_gate(mod, 2) * y, ln_g[l, 2], ln_b[l, 2])
    return x


def setup_inputs(seed=0):
    out = dict(first_inputs(seed))
    for name, value in second_inputs(seed + 1).items():
        if name != "x":
            out[name + "_2"] = value
    return out


def reference(
    x, c, ctx, c_ctx, ada_w, ada_b, norm1_g, norm2_g, w_in, q_norm_g, kv_norm_g, w_uq, w_ukv,
    q_gain, k_gain, conv_w, w_o, w_fourier, ffn_w1, ffn_w3, ffn_w2, c_2, w_ada_2, b_ada_2,
    ln_g_2, ln_b_2, ffn_w_in_2, ffn_w_out_2, mix_w_in_2, pool_w_2, pool_scale_2, rel_bias_2,
    hgrn_lb_2, hgrn_norm_g_2, w_branch_2, w_out_2,
):
    x = first_block(
        x, c, ctx, c_ctx, ada_w, ada_b, norm1_g, norm2_g, w_in, q_norm_g, kv_norm_g, w_uq,
        w_ukv, q_gain, k_gain, conv_w, w_o, w_fourier, ffn_w1, ffn_w3, ffn_w2,
    )
    return second_block(
        x, c_2, w_ada_2, b_ada_2, ln_g_2, ln_b_2, ffn_w_in_2, ffn_w_out_2, mix_w_in_2, pool_w_2,
        pool_scale_2, rel_bias_2, hgrn_lb_2, hgrn_norm_g_2, w_branch_2, w_out_2,
    )


_drawn_inputs = setup_inputs


def setup_inputs(seed=0):
    import zlib

    import numpy as np

    out = dict(_drawn_inputs(seed))
    spreads = {}
    factors = {'ctx': 3.344,
     'norm2_g': 3.248,
     'q_norm_g': 8.0,
     'kv_norm_g': 8.0,
     'q_gain': 8.0,
     'k_gain': 8.0,
     'b_ada_2': 4.918,
     'pool_scale_2': 8.0,
     'hgrn_lb_2': 8.0,
     'hgrn_norm_g_2': 28.252,
     'rel_bias_2': 2.987}
    for name, (base, spread) in spreads.items():
        noise = np.random.default_rng([zlib.crc32(name.encode()), seed]).standard_normal(out[name].shape)
        drawn = base * np.exp(spread * noise) if base else spread * noise
        out[name] = __import__('jax').numpy.asarray(drawn.astype(out[name].dtype))
    for name, factor in factors.items():
        out[name] = (out[name] * factor).astype(out[name].dtype)
    return out
```

```python
from contextlib import ExitStack

import numpy as np
import concourse.bass as bass
from concourse import mybir

ALU = mybir.AluOpType
ACT = mybir.ActivationFunctionType
F32 = mybir.dt.float32
AX = mybir.AxisListType.X

P = 128
T = 256
D = 1024
KD = D // P
TT = T // P
FF = 2816
KF = FF // P
DEPTH = 2

MLA_H, NOPE, ROPE, VD = 8, 64, 32, 64
QKD = NOPE + ROPE
QL, KVL = 384, 256
KQ, KKV = QL // P, KVL // P
CONV = 512
KC = CONV // P
QK_SCALE = QKD ** -0.5

AH, IH = 4, 8
TOPK = 64
BUCKETS, MAX_DIST = 32, 128
HH = 4
KEY_MAX = float(np.float32(1.0 - 1e-6))
ALPHA = (2 * DEPTH) ** 0.25
IDX_SCALE = (64 ** -0.5) * (IH ** -0.5)
AT_SCALE = 64 ** -0.5
TAKEN, UNSEEN = -3.3e38, -3.0e38

SUBS = ["mla", "ffn", "fourier", "ffn", "ffn", "mix", "ffn", "ffn", "mix", "ffn"]
FIRST2 = 4
MODC = 3 * D
ADA_C = 128
ADA_N = MODC // ADA_C

SLOTS = 3
SLOT = 4096
NBANK = 3

HF, HQ, QI, KI, AQ, AK, HG = 0, 4, 8, 12, 13, 15, 17
NPROJ = 21
LEVELS = [64, 32, 16, 8, 4]


HEAD_ORDER = [0, 2, 1, 3]
GATES_AT = [3, 1, 1, 1, 1, 1, 1, 1, 1]

VC, NVEC = {}, 0
for _name, _n in (("norm_g", 32), ("q_norm", 3), ("kv_norm", 2), ("q_gain", 2), ("conv", 12), ("ln_g", 48),
                  ("ln_b", 48), ("pool_scale", 4), ("lb", 8), ("hgrn_norm", 8)):
    VC[_name] = NVEC
    NVEC += _n


class Phase:

    def __init__(self, name, src, nb, cols, first, unit0, per):
        self.name, self.src, self.nb, self.cols, self.first = name, src, nb, cols, first
        self.unit0, self.per = unit0, per


def build(nc, I, out, stop=10, dbg=None):
    subs = SUBS[:stop]
    with ExitStack() as ctx:
        def sb(name, shape):
            return ctx.enter_context(nc.sbuf_tensor(name, shape, F32))

        def sem(name):
            return ctx.enter_context(nc.semaphore(name))

        ring = [sb(f"ring{i}", [P, SLOT]) for i in range(SLOTS)]
        ada_ring = [sb(f"ada_ring{i}", [P, KD, ADA_C]) for i in range(2)]
        ada_sum = sb("ada_sum", [P, MODC])
        x = sb("x", [P, KD, T])
        xc = sb("xc", [P, KD, T])
        sq = sb("sq", [P, KD, T])
        h = sb("h", [P, KD, T])
        big = sb("big", [P, 24, T])
        proj = sb("proj", [P, 24, T])
        rec = sb("rec", [P, 16, T])
        tok = sb("tok", [P, TT, 1024])
        att = sb("att", [P, 8, T])
        yab = sb("yab", [P, 4, T])
        sil = sb("sil", [P, 2, T])
        sd = sb("sd", [P, T])
        rstd = sb("rstd", [P, T])
        bias = sb("bias", [P, AH, TT, T])
        cols = sb("cols", [P, 3, KD])
        csil = sb("csil", [P, 3, KD])
        ada_b = sb("ada_b", [P, 10, 24])
        mod = sb("mod", [P, 24])
        modc = sb("modc", [P, 16])
        vec = sb("vec", [P, NVEC])
        small = sb("small", [P, 64])
        lbv = sb("lbv", [P, 8, HH])
        ones = sb("ones", [P, P])
        eps = sb("eps", [P, 2])
        ident = sb("ident", [P, P])
        masks = sb("masks", [P, 6, P])
        causal = sb("causal", [P, TT, T])
        poolw = sb("poolw", [P, DEPTH, 2, 64])
        work = sb("work", [P, 2, T])
        top8 = sb("top8", [P, 16])

        lin = [ctx.enter_context(nc.psum_tensor(f"lin{i}", [P, 512], F32)) for i in range(NBANK)]
        pstat = ctx.enter_context(nc.psum_tensor("pstat", [P, 512], F32))
        pa = [ctx.enter_context(nc.psum_tensor(f"small_ps{i}", [P, 512], F32)) for i in range(4)]
        bias_rows = nc.dram_tensor("bias_rows", [AH, P * 512 + 512], F32, kind="Internal").ap()

        s_weights = [sem(f"weights_in_slot{i}") for i in range(SLOTS)]
        s_ada_dma = [sem(f"ada_weights_in_slot{i}") for i in range(2)]
        s_unit = sem("units_summed")
        s_taken_by_act, s_taken_by_dve = sem("units_taken_by_act"), sem("units_taken_by_dve")
        s_act_chain = sem("act_chain")
        s_ada_ready = sem("ada_ready")
        s_attended = sem("attended")
        s_attended_taken = sem("attended_taken")
        s_attention_logits = sem("attention_logits")
        s_bias_dma = sem("bias_dma")
        s_bias_row_summed = sem("bias_row_summed")
        s_bias_rows_dma = sem("bias_rows_dma")
        s_bound_exps = sem("bound_exps")
        s_bound_logits = sem("bound_logits")
        s_branches_merged = sem("branches_merged")
        s_cols_dma = sem("cols_dma")
        s_context_ready = sem("context_ready")
        s_conv_done = sem("conv_done")
        s_ctx_dma = sem("ctx_dma")
        s_deviation = sem("deviation")
        s_dve_chain = sem("dve_chain")
        s_exponents = sem("exponents")
        s_far_scores = sem("far_scores")
        s_far_summed = sem("far_summed")
        s_fills = sem("fills")
        s_h_ready = sem("h_ready")
        s_half_turned = sem("half_turned")
        s_head_deviation = sem("head_deviation")
        s_head_normed = sem("head_normed")
        s_head_pair = sem("head_pair")
        s_head_pair_taken = sem("head_pair_taken")
        s_head_squares = sem("head_squares")
        s_head_sum = sem("head_sum")
        s_index_products = sem("index_products")
        s_index_relu = sem("index_relu")
        s_index_relu_used = sem("index_relu_used")
        s_k_rope_part = sem("k_rope_part")
        s_key_capped = sem("key_capped")
        s_latent_deviation = sem("latent_deviation")
        s_latent_squares = sem("latent_squares")
        s_latent_sums = sem("latent_sums")
        s_latents_normed = sem("latents_normed")
        s_level_added = sem("level_added")
        s_level_exps = sem("level_exps")
        s_level_products = sem("level_products")
        s_level_ready = sem("level_ready")
        s_level_scores = sem("level_scores")
        s_log_forget = sem("log_forget")
        s_logits = sem("logits")
        s_logits_exp = sem("logits_exp")
        s_logits_max = sem("logits_max")
        s_mean_sums = sem("mean_sums")
        s_modulation_summed = sem("modulation_summed")
        s_p_normed = sem("p_normed")
        s_p_turned = sem("p_turned")
        s_p_turned_taken = sem("p_turned_taken")
        s_pool_chain = sem("pool_chain")
        s_recurrence_deviation = sem("recurrence_deviation")
        s_recurrence_out = sem("recurrence_out")
        s_recurrence_ready = sem("recurrence_ready")
        s_recurrence_squares = sem("recurrence_squares")
        s_recurrence_sums = sem("recurrence_sums")
        s_result_dma = sem("result_dma")
        s_rope_tables_used = sem("rope_tables_used")
        s_rotated = sem("rotated")
        s_row_exp = sem("row_exp")
        s_row_max = sem("row_max")
        s_rstd_made = sem("rstd_made")
        s_sigmoid_z = sem("sigmoid_z")
        s_silu = sem("silu")
        s_silu_c = sem("silu_c")
        s_silu_q_and_out_gate = sem("silu_q_and_out_gate")
        s_squares = sem("squares")
        s_sums_over_features = sem("sums_over_features")
        s_tables_dma = sem("tables_dma")
        s_weights_ready = sem("weights_ready")
        s_weights_turned = sem("weights_turned")
        s_weights_turned_taken = sem("weights_turned_taken")
        s_x_centred = sem("x_centred")
        s_x_dma = sem("x_dma")
        s_x_new = sem("x_new")
        s_x_summable = sem("x_summable")

        followed = {}

        def nth(eng, s, times=1):
            key = (str(eng.engine), s.num)
            followed[key] = followed.get(key, 0) + times * (16 if s.num in by_dma else 1)
            return followed[key]

        by_dma = {x.num for x in (s_bias_dma, s_bias_rows_dma, s_cols_dma, s_ctx_dma, s_result_dma, s_tables_dma, s_x_dma)}

        phases, takes, unit0, unit_end = [], [], {}, []
        count = {"a": 0, "d": 0}

        def phase(s, name, src, nb, width, units, taker):
            first = phases[-1].first + phases[-1].nb if phases else 0
            phases.append(Phase((s, name), src, nb, width, first, len(takes), units // nb))
            unit_end.extend(len(takes) + (b + 1) * (units // nb) for b in range(nb))
            unit0[s, name] = len(takes)
            for _ in range(units):
                count[taker] += 1
                takes.append((taker, count[taker]))

        nf = nm = 0
        for s, kind in enumerate(subs):
            if kind == "mla":
                phase(s, "in_a", I["w_in_a"], 1, 4096, 3, "a")
                phase(s, "in_b", I["w_in_b"], 1, 1280, 2, "a")
                phase(s, "in_c", I["w_in_c"], 3, 4096, 6, "a")
                phase(s, "uq", I["w_uq"], 1, KQ * MLA_H * QKD, 4, "a")
                phase(s, "ukv", I["w_ukv"], 1, 2048, 12, "a")
                phase(s, "wo", I["w_o"], 2, 4096, 8, "d")
            elif kind == "fourier":
                phase(s, "dft", I["dft"], 1, 2048, 12, "a")
                phase(s, "wf", I["w_f"], 2, 4096, 8, "d")
            elif kind == "ffn":
                phase(s, "w13", I["w13"][nf], KF // 2, 4096, KF, "d")
                phase(s, "w2", I["w2"][nf], KD, FF, KD, "d")
                nf += 1
            else:
                phase(s, "mproj", I["mproj"][nm], 5, 4096, 10, "a")
                phase(s, "mlast", I["mlast"][nm], 1, 1088, 1, "a")
                phase(s, "mtok", I["mtok"][nm], 2, 4096, 4, "a")
                phase(s, "pool", I["poolm"], 1, 2048, 2, "a")
                phase(s, "gates", I["gates"][nm], 6, 4096, 12, "a")
                phase(s, "branch", I["branch"][nm], 2, 4096, 16, "d")
                phase(s, "wout", I["wout"][nm], 2, 4096, 8, "d")
                nm += 1
        by_name = {ph.name: ph for ph in phases}

        def blocks(eng, ph):
            whole = ph.nb // SLOTS if ph.nb >= 2 * SLOTS else 0
            if whole:
                with eng.Fori(0, whole) as i:
                    for j in range(SLOTS):
                        yield i, j
            for b in range(whole * SLOTS, ph.nb):
                yield b // SLOTS, b % SLOTS

        def taken(u):
            who, n = takes[u]
            return (s_taken_by_act if who == "a" else s_taken_by_dve), n

        block = ctx.enter_context(nc.Block())

        @block.sync
        def _(sp):
            sp.dma_start(cols[:], I["cols"]).then_inc(s_cols_dma, 16)
            sp.dma_start(x[:], I["x"]).then_inc(s_x_dma, 16)
            sp.dma_start(rec[:, 8:16], I["ctx"]).then_inc(s_ctx_dma, 16)
            for dst, src in ((vec[:], I["vec"]), (ada_b[:], I["ada_b"]), (ident[:], I["ident"]),
                             (masks[:], I["masks"]), (causal[:], I["causal"]), (poolw[:], I["poolw"]),
                             (bias[0:QKD, 0], I["rope"]), (bias[0:QKD, 1, 0, 0:QKD], I["rot"]),
                             (sil[0:BUCKETS], I["onehot"]), (work[0:BUCKETS], I["relb"])):
                sp.dma_start(dst, src).then_inc(s_tables_dma, 16)

            def load(ph, i, j):
                n, slot = ph.first + j, (ph.first + j) % SLOTS
                if not isinstance(i, int):
                    sp.wait_ge(s_unit, i * SLOTS * ph.per + (ph.unit0 + (j + 1 - SLOTS) * ph.per))
                elif i * SLOTS + n >= SLOTS:
                    sp.wait_ge(s_unit, unit_end[i * SLOTS + n - SLOTS])
                sp.dma_start(ring[slot][:, 0:ph.cols], ph.src[i * SLOTS + j]).then_inc(s_weights[slot], 16)

            for ph in phases:
                whole = ph.nb // SLOTS if ph.nb >= 3 * SLOTS else 1
                for j in range(min(SLOTS, ph.nb)):
                    load(ph, 0, j)
                if whole > 1:
                    with sp.Fori(1, whole) as i:
                        for j in range(SLOTS):
                            load(ph, i, j)
                for b in range(whole * SLOTS, ph.nb):
                    load(ph, b // SLOTS, b % SLOTS)
                if ph.name == (0, "wo"):
                    sp.wait_ge(s_rope_tables_used, nth(sp, s_rope_tables_used))
                    sp.wait_ge(s_bias_rows_dma, nth(sp, s_bias_rows_dma, AH))
                    for a in range(AH):
                        for tt in range(TT):
                            at = 255 - P * tt
                            src = bias_rows[a, at:at + P * 511].rearrange("(p s) -> p s", s=511)[:, 0:T]
                            sp.dma_start(bias[:, a, tt, :], src).then_inc(s_bias_dma, 16)
            sp.wait_ge(s_x_new, nth(sp, s_x_new, len(subs)))
            sp.dma_start(out, x[:]).then_inc(s_result_dma, 16)
            sp.wait_ge(s_result_dma, nth(sp, s_result_dma))

        @block.gpsimd
        def _(pool):
            def load(n):
                if n < ADA_N * len(subs):
                    pool.dma_start(ada_ring[n % 2][:], I["ada"][n]).then_inc(s_ada_dma[n % 2], 16)

            load(0)
            load(1)
            pool.memset(ones[:], 1.0).then_inc(s_fills, 1)
            pool.memset(eps[:, 0:1], 1e-6).then_inc(s_fills, 1)
            pool.memset(eps[:, 1:2], 1e-5).then_inc(s_fills, 1)
            pool.wait_ge(s_silu_c, nth(pool, s_silu_c))

            def product(w, c, dst, into):
                cb = csil[:, c, :].unsqueeze(2).broadcast_to([P, KD, ADA_C])
                pool.tensor_tensor(into, w, cb, ALU.mult).then_inc(s_pool_chain, 1)
                pool.wait_ge(s_pool_chain, nth(pool, s_pool_chain))
                pool.tensor_tensor(into[:, 0:4], into[:, 0:4], into[:, 4:8], ALU.add).then_inc(s_pool_chain, 1)
                pool.wait_ge(s_pool_chain, nth(pool, s_pool_chain))
                pool.tensor_tensor(into[:, 0:2], into[:, 0:2], into[:, 2:4], ALU.add).then_inc(s_pool_chain, 1)
                pool.wait_ge(s_pool_chain, nth(pool, s_pool_chain))
                pool.tensor_tensor(dst, into[:, 0], into[:, 1], ALU.add).then_inc(s_pool_chain, 1)
                pool.wait_ge(s_pool_chain, nth(pool, s_pool_chain))

            spare = big[:, 20:24].rearrange("p a (b c) -> p (a b) c", b=2)
            for s in range(len(subs)):
                if s:
                    pool.wait_ge(s_modulation_summed, nth(pool, s_modulation_summed))
                for b in range(ADA_N):
                    n = s * ADA_N + b
                    pool.wait_ge(s_ada_dma[n % 2], (n // 2 + 1) * 16)
                    w = ada_ring[n % 2][:]
                    if s == 0 and b < 2 * D // ADA_C:
                        product(w, 1, big[:, b // 2, (b % 2) * P:(b % 2) * P + P], spare)
                    product(w, 0 if s < FIRST2 else 2, ada_sum[:, b * ADA_C:(b + 1) * ADA_C], w)
                    load(n + 2)
                pool.sem_inc(s_ada_ready, 1)

        @block.scalar
        def _(act):
            A = nc.scalar.activation

            def take(u, pairs):
                act.wait_ge(s_unit, (u) + 1)
                for dst, lo, hi, p0, p1 in pairs:
                    src = lin[u % NBANK][p0:p1, lo:hi]
                    if len(dst.shape) == 3:
                        src = src.rearrange("p (a b) -> p a b", a=dst.shape[1])
                    ins = A(dst, src, ACT.Copy)
                ins.then_inc(s_taken_by_act, 1)

            act.wait_ge(s_cols_dma, nth(act, s_cols_dma))
            A(csil[:], cols[:], ACT.Silu).then_inc(s_silu_c, 1)
            act.wait_ge(s_fills, nth(act, s_fills, 3))
            act.wait_ge(s_bound_logits, nth(act, s_bound_logits))
            A(lbv[:, 1:3], lbv[:, 1:3], ACT.Exp).then_inc(s_bound_exps, 1)

            for a in range(AH):
                act.wait_ge(s_bias_row_summed, nth(act, s_bias_row_summed))
                rows = tok[:].rearrange("p a b -> p (a b)")[:, a * 512:(a + 1) * 512]
                A(rows, pa[a][:], ACT.Copy).then_inc(s_act_chain, 1)
                act.wait_ge(s_act_chain, nth(act, s_act_chain))
                act.dma_start(bias_rows[a, 0:P * 512].rearrange("(p s) -> p s", s=512), rows)\
                   .then_inc(s_bias_rows_dma, 16)

            def deviation(e=0):
                act.wait_ge(s_sums_over_features, nth(act, s_sums_over_features))
                A(sd[:], pstat[:, 0:T], ACT.Sqrt, scale=1.0 / D, bias=eps[:, e:e + 1]).then_inc(s_deviation, 1)

            def squares(dst, src):
                for k in range(0, KD, 4):
                    A(dst[:, k:k + 4], src[:, k:k + 4], ACT.Square).then_inc(s_squares, 1)

            def col(name, n=0):
                return vec[:, VC[name] + n:VC[name] + n + 1]

            def mix(s):
                l = subs[:s].count("mix")
                u = unit0[s, "mproj"]
                for n in range(10):
                    take(u + n, [(proj[:, 2 * n:2 * n + 2], 0, 512, 0, P)])
                take(u + 10, [(proj[:, 20], 0, T, 0, P), (small[:, 0:TT * IH], T, T + TT * IH, 0, P)])
                for n in range(4):
                    take(u + 11 + n, [(tok[:, n % 2, (n // 2) * 512:(n // 2) * 512 + 512], 0, 512, 0, P)])
                take(u + 15, [(work[:], 0, 512, 0, P)])
                A(rec[:, 0:4], proj[:, HF:HF + 4], ACT.Sigmoid, scale=-1.0).then_inc(s_sigmoid_z, 1)
                A(proj[:, HQ:HQ + 4], proj[:, HQ:HQ + 4], ACT.Silu).then_inc(s_act_chain, 1)
                act.wait_ge(s_act_chain, nth(act, s_act_chain))
                A(proj[:, HG:HG + 4], proj[:, HG:HG + 4], ACT.Silu).then_inc(s_silu_q_and_out_gate, 1)
                act.wait_ge(s_silu_q_and_out_gate, nth(act, s_silu_q_and_out_gate))
                act.wait_ge(s_key_capped, nth(act, s_key_capped))
                A(proj[:, HF:HF + 4], proj[:, HF:HF + 4], ACT.Ln, scale=-1.0, bias=1.0).then_inc(s_log_forget, 1)
                for n in range(TT * IH // 2):
                    act.wait_ge(s_index_products, nth(act, s_index_products))
                    if n >= 2:
                        act.wait_ge(s_index_relu_used, nth(act, s_index_relu_used))
                    A(att[:, 2 * (n % 2):2 * (n % 2) + 2],
                      pa[n % 4][:].rearrange("p (a b) -> p a b", a=2), ACT.Relu).then_inc(s_index_relu, 1)
                act.wait_ge(s_unit, (u + 16) + 1)
                for i in range(2):
                    ps = col("pool_scale", 2 * l + i)
                    ins = A(yab[:, i], lin[(u + 16) % NBANK][:, i * T:i * T + T], ACT.Copy, scale=ps)
                ins.then_inc(s_taken_by_act, 1)
                g = [0]

                def gate_units(n):
                    for _ in range(n):
                        m = g[0]
                        g[0] += 1
                        act.wait_ge(s_unit, (u + 17 + m) + 1)
                        A(big[:, 2 * m:2 * m + 2],
                          lin[(u + 17 + m) % NBANK][:].rearrange("p (a b) -> p a b", a=2),
                          ACT.Sigmoid).then_inc(s_taken_by_act, 1)

                def exp_level(n):
                    act.wait_ge(s_exponents, nth(act, s_exponents))
                    A(xc[:, 4:8], xc[:, 0:4], ACT.Exp).then_inc(s_level_exps, 1)
                    if n == 6:
                        A(xc[:, 0:4], xc[:, 0:4], ACT.Exp, scale=-1.0).then_inc(s_level_exps, 1)

                gate_units(GATES_AT[0])
                act.wait_ge(s_index_relu_used, nth(act, s_index_relu_used, 2))
                exp_level(0)
                act.wait_ge(s_far_summed, nth(act, s_far_summed))
                A(sq[:, 4:6], pa[0][:].rearrange("p (a b) -> p a b", a=2), ACT.Copy).then_inc(s_far_scores, 1)
                for n in range(1, 7):
                    exp_level(n)
                    gate_units(GATES_AT[n])
                for tt in range(TT):
                    act.wait_ge(s_logits_max, nth(act, s_logits_max))
                    for a in range(AH):
                        ins = A(att[:, a], att[:, a], ACT.Exp, bias=small[:, 24 + a:25 + a],
                                accum_out=small[:, 28 + a:29 + a])
                    ins.then_inc(s_logits_exp, 1)
                    act.wait_ge(s_weights_turned, nth(act, s_weights_turned))
                    for kt in range(TT):
                        ins = A(att[:, 4 + 2 * kt:6 + 2 * kt], pa[2 * tt + kt][:].rearrange("p (a b) -> p a b", a=2),
                                ACT.Copy)
                    ins.then_inc(s_weights_turned_taken, 1)
                    act.wait_ge(s_attended, nth(act, s_attended))
                    ins = A(yab[:, 2:4, tt * P:tt * P + P], pstat[:, 0:T].rearrange("p (a b) -> p a b", a=2), ACT.Copy)
                    ins.then_inc(s_attended_taken, 1)
                    gate_units(GATES_AT[7 + tt])
                for tt in range(TT):
                    act.wait_ge(s_recurrence_out, nth(act, s_recurrence_out))
                    A(rec[:, 0:4, tt * P:tt * P + P], pa[tt][:].rearrange("p (a b) -> p a b", a=4), ACT.Copy).then_inc(s_act_chain, 1)
                    act.wait_ge(s_act_chain, nth(act, s_act_chain))
                A(rec[:, 4:8], rec[:, 0:4], ACT.Square).then_inc(s_recurrence_squares, 1)
                for n in range(2):
                    act.wait_ge(s_recurrence_sums, nth(act, s_recurrence_sums))
                    ins = A(rec[:, 8 + 2 * n:10 + 2 * n], pa[2 + n][:].rearrange("p (a b) -> p a b", a=2), ACT.Sqrt,
                            scale=1.0 / P, bias=eps[:, 0:1])
                ins.then_inc(s_recurrence_deviation, 1)
                gate_units(12 - g[0])

            for s, kind in enumerate(subs):
                if s == 0:
                    act.wait_ge(s_x_dma, nth(act, s_x_dma))
                    act.wait_ge(s_ctx_dma, nth(act, s_ctx_dma))
                else:
                    act.wait_ge(s_x_new, nth(act, s_x_new))
                if s < FIRST2:
                    squares(sq, x)
                    deviation()
                if kind == "mla":
                    squares(sq, rec[:, 8:16])
                    act.wait_ge(s_rstd_made, nth(act, s_rstd_made))
                    deviation()
                    cq, ckv = proj[:, 12:15], proj[:, 15:19]
                    kpe = proj[64:96, 19:21]
                    u = unit0[s, "in_a"]
                    take(u, [(cq[:, 0:2], 0, 512, 0, P)])
                    take(u + 1, [(cq[:, 2], 0, T, 0, P)])
                    take(u + 2, [(ckv[:, 0:2], 0, 512, 0, P)])
                    take(u + 3, [(ckv[:, 2:4], 0, 512, 0, P)])
                    take(u + 4, [(kpe, 0, 512, 64, 96)])
                    A(sq[:, 0:3], cq, ACT.Square).then_inc(s_act_chain, 1)
                    act.wait_ge(s_act_chain, nth(act, s_act_chain))
                    A(sq[:, 3:7], ckv, ACT.Square).then_inc(s_latent_squares, 1)
                    for n in range(6):
                        take(u + 5 + n, [(proj[:, 2 * n:2 * n + 2], 0, 512, 0, P)])
                    act.wait_ge(s_latent_sums, nth(act, s_latent_sums))
                    A(sq[:, 0], pstat[:, 0:T], ACT.Sqrt, scale=1.0 / QL, bias=eps[:, 0:1])
                    A(sq[:, 1:3], pa[0][:].rearrange("p (a b) -> p a b", a=2), ACT.Sqrt,
                      scale=1.0 / KVL, bias=eps[:, 0:1]).then_inc(s_latent_deviation, 1)
                    qh = big[0:QKD, 16:24]
                    kh = big[:, 0:16].rearrange("p (h t) c -> p h (t c)", t=2)
                    u = unit0[s, "uq"]
                    for n in range(4):
                        take(u + n, [(qh[:, 2 * n:2 * n + 2], 0, 512, 0, QKD)])
                    for n in range(MLA_H):
                        take(u + 4 + n, [(kh[0:NOPE, n], 0, 512, 0, NOPE)])
                    act.wait_ge(s_bias_rows_dma, nth(act, s_bias_rows_dma, AH))
                    vt = tok[:].rearrange("p a (b c) -> p (a b) c", c=512)
                    for n in range(4):
                        take(u + 12 + n, [(vt[:, n], 0, 512, 0, P)])
                    act.wait_ge(s_latents_normed, nth(act, s_latents_normed))
                    A(sq[0:QKD], qh, ACT.Square).then_inc(s_act_chain, 1)
                    act.wait_ge(s_act_chain, nth(act, s_act_chain))
                    act.wait_ge(s_k_rope_part, nth(act, s_k_rope_part))
                    act.wait_ge(s_conv_done, nth(act, s_conv_done))
                    A(rec[0:QKD], big[0:QKD, 0:16], ACT.Square).then_inc(s_head_squares, 1)
                    for n in range(12):
                        act.wait_ge(s_head_sum, nth(act, s_head_sum))
                        dst = sq[0:QKD, 2 * n:2 * n + 2] if n < 4 else rec[0:QKD, 2 * n - 8:2 * n - 6]
                        A(dst, pa[n % 4][0:QKD].rearrange("p (a b) -> p a b", a=2), ACT.Sqrt,
                          scale=1.0 / QKD, bias=eps[0:QKD, 0:1]).then_inc(s_head_deviation, 1)
                    for n in range(2 * MLA_H + 1):
                        if n < 2 * MLA_H:
                            act.wait_ge(s_row_max, nth(act, s_row_max))
                            p = sq[:, 2 * (n % 2):2 * (n % 2) + 2].rearrange("p a b -> p (a b)")
                            A(p, pa[n % 2][:], ACT.Exp, scale=QK_SCALE,
                              bias=small[:, 16 + n % 2:17 + n % 2],
                              accum_out=small[:, 18 + n % 2:19 + n % 2]).then_inc(s_row_exp, 1)
                        if n:
                            m = n - 1
                            act.wait_ge(s_p_turned, nth(act, s_p_turned))
                            A(sq[:, 4 + 2 * (m % 2):6 + 2 * (m % 2)],
                              pa[2][:].rearrange("p (a b) -> p a b", a=2), ACT.Copy).then_inc(s_p_turned_taken, 1)
                        if n > 1 and (n - 2) % 4 == 3:
                            pair = (n - 2) // 4
                            act.wait_ge(s_head_pair, nth(act, s_head_pair))
                            A(h[:, pair], (pa[3], pstat)[pair % 2][:, 0:T], ACT.Copy).then_inc(s_head_pair_taken, 1)
                    act.wait_ge(s_head_pair, nth(act, s_head_pair))
                    A(h[:, 3], pstat[:, 0:T], ACT.Copy).then_inc(s_head_pair_taken, 1)
                if kind == "ffn":
                    u0 = unit0[s, "w13"]
                    for i, j in blocks(act, by_name[s, "w13"]):
                        for c in range(2):
                            n = 2 * j + c
                            act.wait_ge(s_unit, (i * 2 * SLOTS + (u0 + n)) + 1)
                            act.wait_ge(s_taken_by_dve, i * 2 * SLOTS + (takes[u0 + n][1] - 2))
                            A(sil[:, n % 2], lin[(u0 + n) % NBANK][:, 0:T], ACT.Silu).then_inc(s_silu, 1)
                if kind == "fourier":
                    u = unit0[s, "dft"]
                    for n in range(8):
                        take(u + n, [(big[:, 2 * n:2 * n + 2], 0, 512, 0, P)])
                    for n in range(4):
                        take(u + 8 + n, [(h[:, 2 * n:2 * n + 2], 0, 512, 0, P)])
                if kind == "mix":
                    mix(s)
                if s >= FIRST2:
                    for k in range(0, KD, 4):
                        act.wait_ge(s_x_centred, nth(act, s_x_centred))
                        A(sq[:, k:k + 4], xc[:, k:k + 4], ACT.Square).then_inc(s_squares, 1)
                    deviation(1)
        @block.vector
        def _(dve):
            V = nc.vector

            def col(name, n=0):
                return vec[:, VC[name] + n:VC[name] + n + 1]

            def modulation(s):
                dve.wait_ge(s_modulation_summed, nth(dve, s_modulation_summed))
                V.tensor_tensor(mod[:], pa[3][:, 0:24], ada_b[:, s], ALU.add).then_inc(s_dve_chain, 1)
                dve.wait_ge(s_dve_chain, nth(dve, s_dve_chain))
                scale, gate = mod[:, 8:16], mod[:, 16:24]
                if s < FIRST2:
                    g = vec[:, VC["norm_g"] + 8 * s:VC["norm_g"] + 8 * s + 8]
                    if s == 0:
                        V.tensor_tensor(modc[:], pa[3][:, 32:48], ada_b[:, s, 0:16], ALU.add).then_inc(s_dve_chain, 1)
                        dve.wait_ge(s_dve_chain, nth(dve, s_dve_chain))
                        V.scalar_tensor_tensor(modc[:, 8:16], modc[:, 8:16], 1.0, g, ALU.add, ALU.mult).then_inc(s_dve_chain, 1)
                        dve.wait_ge(s_dve_chain, nth(dve, s_dve_chain))
                    V.scalar_tensor_tensor(scale, scale, 1.0, g, ALU.add, ALU.mult).then_inc(s_dve_chain, 1)
                    dve.wait_ge(s_dve_chain, nth(dve, s_dve_chain))
                else:
                    V.tensor_scalar(scale, scale, 1.0, None, ALU.add).then_inc(s_dve_chain, 1)
                    dve.wait_ge(s_dve_chain, nth(dve, s_dve_chain))
                    V.tensor_scalar(gate, gate, 1.0, 0.5 if subs[s] == "ffn" else 1.0, ALU.add, ALU.mult).then_inc(s_dve_chain, 1)
                    dve.wait_ge(s_dve_chain, nth(dve, s_dve_chain))

            def by_rstd(src, dst, e=0):
                dve.wait_ge(s_deviation, nth(dve, s_deviation))
                V.reciprocal(rstd[:], sd[:]).then_inc(s_dve_chain, 1)
                dve.wait_ge(s_dve_chain, nth(dve, s_dve_chain))
                V.tensor_tensor(dst, src, rstd[:].unsqueeze(1).broadcast_to([P, KD, T]), ALU.mult).then_inc(s_rstd_made, 1)
                dve.wait_ge(s_rstd_made, nth(dve, s_rstd_made))

            def affine(dst, src, a, b):
                for k in range(KD):
                    ins = V.tensor_scalar(dst[:, k], src[:, k], a[:, k:k + 1], b[:, k:k + 1], ALU.mult, ALU.add)
                return ins

            def residual(s, name):
                u0 = unit0[s, name]
                ph = by_name[s, name]
                per = KD // ph.nb
                for i, j in blocks(dve, ph):
                    for c in range(per):
                        n = j * per + c
                        dve.wait_ge(s_unit, (i * SLOTS * per + (u0 + n)) + 1)
                        m = i * SLOTS * per + n
                        gate = mod[:, 16 + m:17 + m] if isinstance(m, int) else mod[:, bass.ds(m + 16, 1)]
                        xt = x[:, m] if isinstance(m, int) else x[:, bass.ds(m, 1), :].rearrange("p a b -> p (a b)")
                        ins = V.scalar_tensor_tensor(xt, lin[(u0 + n) % NBANK][:, 0:T], gate, xt, ALU.mult, ALU.add)
                        ins.then_inc(s_taken_by_dve, 1)
                dve.wait_ge(*taken(u0 + KD - 1))

            def mla(s):
                cq, ckv = proj[:, 12:15], proj[:, 15:19]
                dve.wait_ge(s_latent_deviation, nth(dve, s_latent_deviation))
                V.reciprocal(sq[:, 0:3], sq[:, 0:3]).then_inc(s_dve_chain, 1)
                dve.wait_ge(s_dve_chain, nth(dve, s_dve_chain))
                for k in range(KQ):
                    V.scalar_tensor_tensor(cq[:, k], cq[:, k], col("q_norm", k), sq[:, 0], ALU.mult, ALU.mult)
                for k in range(KKV):
                    kv = ckv[:, 2 * k:2 * k + 2]
                    ins = V.scalar_tensor_tensor(kv, kv, col("kv_norm", k), sq[:, 1:3], ALU.mult, ALU.mult)
                ins.then_inc(s_latents_normed, 1)
                u = unit0[s, "in_a"]
                dve.wait_ge(*taken(u + 4))
                kh = big[:, 0:16].rearrange("p (h t) c -> p h (t c)", t=2)
                kpe = proj[64:96, 19:21].rearrange("p a b -> p (a b)").unsqueeze(1).broadcast_to([ROPE, MLA_H, 2 * T])
                V.tensor_copy(kh[64:96], kpe).then_inc(s_k_rope_part, 1)
                dve.wait_ge(*taken(u + 10))
                zp = rec[:].rearrange("p a b -> p (a b)")[:, 0:KC * (T + 2)].rearrange("p (k t) -> p k t", k=KC)
                y = rec[:, 8:12]
                V.memset(zp[:, :, 0:1], 0.0).then_inc(s_dve_chain, 1)
                dve.wait_ge(s_dve_chain, nth(dve, s_dve_chain))
                V.memset(zp[:, :, T + 1:T + 2], 0.0).then_inc(s_dve_chain, 1)
                dve.wait_ge(s_dve_chain, nth(dve, s_dve_chain))
                V.tensor_tensor(zp[:, :, 1:T + 1], proj[:, 4:8], proj[:, 8:12], ALU.mult).then_inc(s_dve_chain, 1)
                dve.wait_ge(s_dve_chain, nth(dve, s_dve_chain))
                for k in range(KC):
                    ins = V.tensor_scalar(y[:, k], zp[:, k, 0:T], col("conv", k), None, ALU.mult)
                ins.then_inc(s_dve_chain, 1)
                dve.wait_ge(s_dve_chain, nth(dve, s_dve_chain))
                for w in (1, 2):
                    for k in range(KC):
                        ins = V.scalar_tensor_tensor(y[:, k], zp[:, k, w:w + T], col("conv", w * KC + k), y[:, k],
                                                     ALU.mult, ALU.add)
                    ins.then_inc(s_dve_chain, 1)
                    dve.wait_ge(s_dve_chain, nth(dve, s_dve_chain))
                V.tensor_tensor(h[:, 4:8], proj[:, 0:4], y, ALU.mult).then_inc(s_conv_done, 1)
                for n in range(12):
                    dve.wait_ge(s_head_deviation, nth(dve, s_head_deviation))
                    r = sq[0:QKD, 2 * n:2 * n + 2] if n < 4 else rec[0:QKD, 2 * n - 8:2 * n - 6]
                    v = big[0:QKD, 16 + 2 * n:18 + 2 * n] if n < 4 else big[0:QKD, 2 * n - 8:2 * n - 6]
                    V.reciprocal(r, r).then_inc(s_dve_chain, 1)
                    dve.wait_ge(s_dve_chain, nth(dve, s_dve_chain))
                    gain = vec[0:QKD, VC["q_gain"] + (n >= 4):VC["q_gain"] + (n >= 4) + 1]
                    V.scalar_tensor_tensor(v, v, gain, r, ALU.mult, ALU.mult).then_inc(s_head_normed, 1)
                cos = bias[64:96, 0, 0].unsqueeze(1).broadcast_to([ROPE, 2, T])
                sin = bias[64:96, 0, 1].unsqueeze(1).broadcast_to([ROPE, 2, T])
                dve.wait_ge(s_head_normed, nth(dve, s_head_normed, 12))
                for n in range(8):
                    dve.wait_ge(s_half_turned, nth(dve, s_half_turned))
                    v = big[64:96, 16 + 2 * n:18 + 2 * n] if n < 4 else big[64:96, 4 * (n - 4):4 * (n - 4) + 3:2]
                    t = sq[64:96, 0:2]
                    ps = pa[n % 4][64:96].rearrange("p (a b) -> p a b", a=2)
                    V.tensor_tensor(t, ps, sin, ALU.mult)
                    V.tensor_tensor(v, v, cos, ALU.mult).then_inc(s_dve_chain, 1)
                    dve.wait_ge(s_dve_chain, nth(dve, s_dve_chain))
                    V.tensor_tensor(v, v, t, ALU.add).then_inc(s_rotated, 1)
                    dve.wait_ge(s_rotated, nth(dve, s_rotated))
                dve.sem_inc(s_rope_tables_used, 1)
                for n in range(2 * MLA_H + 1):
                    if n < 2 * MLA_H:
                        dve.wait_ge(s_logits, nth(dve, s_logits))
                        V.tensor_reduce(small[:, 20 + n % 2:21 + n % 2], pa[n % 2][:], AX, ALU.max, negate=True).then_inc(s_dve_chain, 1)
                        dve.wait_ge(s_dve_chain, nth(dve, s_dve_chain))
                        V.tensor_scalar(small[:, 16 + n % 2:17 + n % 2],
                                        small[:, 20 + n % 2:21 + n % 2], QK_SCALE, None, ALU.mult).then_inc(s_row_max, 1)
                    if n:
                        m = (n - 1) % 2
                        dve.wait_ge(s_row_exp, nth(dve, s_row_exp))
                        V.reciprocal(small[:, 22 + m:23 + m], small[:, 18 + m:19 + m]).then_inc(s_dve_chain, 1)
                        dve.wait_ge(s_dve_chain, nth(dve, s_dve_chain))
                        p = sq[:, 2 * m:2 * m + 2]
                        V.tensor_scalar(p, p, small[:, 22 + m:23 + m], None, ALU.mult).then_inc(s_p_normed, 1)

            def mix(s):
                l = subs[:s].count("mix")
                key, run, q_l, k_l = rec[:, 0:4], rec[:, 4:8], rec[:, 8:12], rec[:, 12:16]
                dve.wait_ge(s_sigmoid_z, nth(dve, s_sigmoid_z))
                for a in range(HH):
                    ins = V.tensor_scalar(key[:, a], key[:, a], lbv[:, 6 + l, a:a + 1], None, ALU.mult)
                ins.then_inc(s_dve_chain, 1)
                dve.wait_ge(s_dve_chain, nth(dve, s_dve_chain))
                V.tensor_scalar(proj[:, HF:HF + 4], key, KEY_MAX, None, ALU.min).then_inc(s_key_capped, 1)
                V.memset(rec[:, 8:16], 0.0).then_inc(s_dve_chain, 1)
                dve.wait_ge(s_dve_chain, nth(dve, s_dve_chain))
                dve.wait_ge(s_log_forget, nth(dve, s_log_forget))
                for a in range(HH):
                    ins = V.tensor_tensor_scan(run[:, a], ones[:, 0:1].broadcast_to([P, T]), proj[:, HF + a], 0.0,
                                               ALU.mult, ALU.add)
                ins.then_inc(s_dve_chain, 1)
                dve.wait_ge(s_dve_chain, nth(dve, s_dve_chain))
                for n in range(TT * IH // 2):
                    dve.wait_ge(s_index_relu, nth(dve, s_index_relu))
                    tt, acc = n // 4, sil[:, n // 4]
                    for c in range(2):
                        r = att[:, 2 * (n % 2) + c]
                        head = tt * IH + 4 * (n % 4 // 2) + 2 * c + n % 2
                        w = small[:, head:head + 1]
                        if n % 4 == 0 and c == 0:
                            V.tensor_scalar(acc, r, w, None, ALU.mult).then_inc(s_dve_chain, 1)
                            dve.wait_ge(s_dve_chain, nth(dve, s_dve_chain))
                        elif c == 0:
                            V.scalar_tensor_tensor(acc, r, w, acc, ALU.mult, ALU.add).then_inc(s_dve_chain, 1)
                            dve.wait_ge(s_dve_chain, nth(dve, s_dve_chain))
                        else:
                            V.scalar_tensor_tensor(acc, r, w, acc, ALU.mult, ALU.add).then_inc(s_index_relu_used, 1)
                            dve.wait_ge(s_index_relu_used, nth(dve, s_index_relu_used))
                dve.wait_ge(s_unit, (unit0[s, "pool"] + 1) + 1)
                V.tensor_scalar(work[:], causal[:], -1.0, -UNSEEN, ALU.add, ALU.mult).then_inc(s_dve_chain, 1)
                dve.wait_ge(s_dve_chain, nth(dve, s_dve_chain))
                V.scalar_tensor_tensor(sil[:], sil[:], IDX_SCALE, causal[:], ALU.mult, ALU.mult).then_inc(s_dve_chain, 1)
                dve.wait_ge(s_dve_chain, nth(dve, s_dve_chain))
                V.tensor_tensor(sil[:], sil[:], work[:], ALU.add).then_inc(s_dve_chain, 1)
                dve.wait_ge(s_dve_chain, nth(dve, s_dve_chain))
                for r in range(TOPK // 8):
                    for tt in range(TT):
                        src = sil[:, tt] if r == 0 else work[:, tt]
                        V.max(top8[:, 8 * tt:8 * tt + 8], src).then_inc(s_dve_chain, 1)
                        dve.wait_ge(s_dve_chain, nth(dve, s_dve_chain))
                        V.match_replace(work[:, tt], top8[:, 8 * tt:8 * tt + 8], src, TAKEN).then_inc(s_dve_chain, 1)
                        dve.wait_ge(s_dve_chain, nth(dve, s_dve_chain))
                V.scalar_tensor_tensor(sil[:], work[:], TAKEN, causal[:], ALU.is_equal, ALU.mult).then_inc(s_dve_chain, 1)
                dve.wait_ge(s_dve_chain, nth(dve, s_dve_chain))
                V.tensor_scalar(sil[:], sil[:], -1.0, 1e30, ALU.add, ALU.mult).then_inc(s_dve_chain, 1)
                dve.wait_ge(s_dve_chain, nth(dve, s_dve_chain))

                dve.wait_ge(s_silu_q_and_out_gate, nth(dve, s_silu_q_and_out_gate))
                q = proj[:, HQ:HQ + 4]

                def halves(v, m):
                    return v.rearrange("p a b -> p (a b)").rearrange("p (b r) -> p b r", r=2 * m)

                def exponents(n):
                    d = xc[:, 0:4]
                    if n < 6:
                        m = ([P] + LEVELS)[n]
                        a, e = halves(run, m), halves(d, m)
                        mid = a[:, :, m - 1:m].broadcast_to([P, a.shape[1], m])
                        V.tensor_tensor(e[:, :, 0:m], mid, a[:, :, 0:m], ALU.subtract)
                        V.tensor_tensor(e[:, :, m:2 * m], a[:, :, m:2 * m], mid, ALU.subtract).then_inc(s_exponents, 1)
                    else:
                        a, e = halves(run, 2), halves(d, 2)
                        mid = a[:, :, 1:2].broadcast_to([P, a.shape[1], 4])
                        V.tensor_tensor(e, a, mid, ALU.subtract).then_inc(s_exponents, 1)

                def add_level(n):
                    for tt in range(TT):
                        dve.wait_ge(s_level_scores, nth(dve, s_level_scores))
                        ps = pa[2 * (n % 2) + tt][:].rearrange("p (a b) -> p a b", a=HH)
                        mask = masks[:, n - 1].unsqueeze(1).broadcast_to([P, HH, P])
                        acc, t = sq[:, 2 * tt:2 * tt + 2], sq[:, 6:8]
                        four = lambda v: v.rearrange("p a b -> p (a b)").rearrange("p (a b) -> p a b", a=HH)
                        if n == 1:
                            V.tensor_tensor(four(acc), ps, mask, ALU.mult).then_inc(s_level_added, 1)
                            dve.wait_ge(s_level_added, nth(dve, s_level_added))
                        else:
                            V.tensor_tensor(four(t), ps, mask, ALU.mult).then_inc(s_dve_chain, 1)
                            dve.wait_ge(s_dve_chain, nth(dve, s_dve_chain))
                            V.tensor_tensor(acc, acc, t, ALU.add).then_inc(s_level_added, 1)
                            dve.wait_ge(s_level_added, nth(dve, s_level_added))

                exponents(0)
                for n in range(7):
                    dve.wait_ge(s_level_exps, nth(dve, s_level_exps, 2 if n == 6 else 1))
                    if n:
                        dve.wait_ge(s_level_products, nth(dve, s_level_products))
                    if n < 6:
                        m = ([P] + LEVELS)[n]
                        e = halves(xc[:, 4:8], m)
                        V.tensor_tensor(halves(q_l, m)[:, :, m:2 * m], halves(q, m)[:, :, m:2 * m], e[:, :, m:2 * m],
                                        ALU.mult)
                        V.tensor_tensor(halves(k_l, m)[:, :, 0:m], halves(key, m)[:, :, 0:m],
                                        e[:, :, 0:m], ALU.mult).then_inc(s_level_ready, 1)
                        exponents(n + 1)
                    else:
                        V.tensor_tensor(q_l, q, xc[:, 4:8], ALU.mult)
                        V.tensor_tensor(k_l, key, xc[:, 0:4], ALU.mult).then_inc(s_level_ready, 1)
                    if n > 1:
                        add_level(n - 1)
                dve.wait_ge(s_level_products, nth(dve, s_level_products))
                add_level(6)

                if l == 0:
                    dve.wait_ge(s_bias_dma, nth(dve, s_bias_dma, AH * TT))
                for tt in range(TT):
                    lg = att[:, 0:4]
                    if tt:
                        dve.wait_ge(s_weights_turned_taken, nth(dve, s_weights_turned_taken))
                    for pair in range(2):
                        dve.wait_ge(s_attention_logits, nth(dve, s_attention_logits))
                        ps = pa[2 * tt + pair][:].rearrange("p (a b) -> p a b", a=2)
                        ins = V.scalar_tensor_tensor(lg[:, 2 * pair:2 * pair + 2], ps, AT_SCALE,
                                                     bias[:, pair:pair + 3:2, tt], ALU.mult, ALU.add)
                    ins.then_inc(s_dve_chain, 1)
                    dve.wait_ge(s_dve_chain, nth(dve, s_dve_chain))
                    V.tensor_tensor(lg, lg, sil[:, tt].unsqueeze(1).broadcast_to([P, AH, T]), ALU.add).then_inc(s_dve_chain, 1)
                    dve.wait_ge(s_dve_chain, nth(dve, s_dve_chain))
                    V.tensor_reduce(small[:, 24:28], lg, AX, ALU.max, negate=True).then_inc(s_logits_max, 1)
                    dve.wait_ge(s_logits_exp, nth(dve, s_logits_exp))
                    V.reciprocal(small[:, 32:36], small[:, 28:32]).then_inc(s_dve_chain, 1)
                    dve.wait_ge(s_dve_chain, nth(dve, s_dve_chain))
                    V.tensor_tensor(
 lg, lg, small[:, 32:36].unsqueeze(2).broadcast_to([P, AH, T]), ALU.mult).then_inc(s_weights_ready, 1)

                dve.wait_ge(s_recurrence_deviation, nth(dve, s_recurrence_deviation))
                o, r = rec[:, 0:4], rec[:, 8:12]
                V.reciprocal(r, r).then_inc(s_dve_chain, 1)
                dve.wait_ge(s_dve_chain, nth(dve, s_dve_chain))
                V.tensor_tensor(o, o, r, ALU.mult).then_inc(s_dve_chain, 1)
                dve.wait_ge(s_dve_chain, nth(dve, s_dve_chain))
                for a in range(HH):
                    ins = V.scalar_tensor_tensor(o[:, a], o[:, a], col("hgrn_norm", l * HH + a), proj[:, HG + a],
                                                 ALU.mult, ALU.mult)
                ins.then_inc(s_recurrence_ready, 1)
                dve.wait_ge(s_attended_taken, nth(dve, s_attended_taken, 2))
                dve.wait_ge(s_weights_turned_taken, nth(dve, s_weights_turned_taken))

                u = unit0[s, "branch"]
                for m in range(KD):
                    dve.wait_ge(s_unit, (u + 2 * m) + 1)
                    if m == 0:
                        dve.wait_ge(*taken(u - 1))
                    t = att[:, 0:2]
                    gates = big[:, m:m + KD + 1:KD]
                    V.tensor_tensor(t, lin[(u + 2 * m) % NBANK][:].rearrange("p (a b) -> p a b", a=2),
                                    gates, ALU.mult).then_inc(s_taken_by_dve, 1)
                    dve.wait_ge(s_unit, (u + 2 * m + 1) + 1)
                    V.tensor_tensor(att[:, 2], lin[(u + 2 * m + 1) % NBANK][:, 0:T],
                                    big[:, 2 * KD + m], ALU.mult).then_inc(s_taken_by_dve, 1)
                    dve.wait_ge(*taken(u + 2 * m + 1))
                    V.tensor_tensor(att[:, 0], att[:, 0], att[:, 1], ALU.add).then_inc(s_dve_chain, 1)
                    dve.wait_ge(s_dve_chain, nth(dve, s_dve_chain))
                    ins = V.tensor_tensor(h[:, m], att[:, 0], att[:, 2], ALU.add)
                    ins.then_inc(s_branches_merged, 1)
                    dve.wait_ge(s_branches_merged, nth(dve, s_branches_merged))

            dve.wait_ge(s_tables_dma, nth(dve, s_tables_dma, 10))
            dve.wait_ge(s_x_dma, nth(dve, s_x_dma))
            lb = [vec[:, VC["lb"] + HH * l:VC["lb"] + HH * l + HH] for l in range(DEPTH)]
            V.tensor_tensor(lbv[:, 0], lb[0], lb[1], ALU.max).then_inc(s_dve_chain, 1)
            dve.wait_ge(s_dve_chain, nth(dve, s_dve_chain))
            V.tensor_tensor(lbv[:, 1], lb[0], lbv[:, 0], ALU.subtract).then_inc(s_dve_chain, 1)
            dve.wait_ge(s_dve_chain, nth(dve, s_dve_chain))
            V.tensor_tensor(lbv[:, 2], lb[1], lbv[:, 0], ALU.subtract).then_inc(s_dve_chain, 1)
            dve.wait_ge(s_dve_chain, nth(dve, s_dve_chain))
            V.tensor_copy(lbv[:, 3], lbv[:, 0]).then_inc(s_bound_logits, 1)
            dve.wait_ge(s_bound_exps, nth(dve, s_bound_exps))
            V.tensor_tensor(lbv[:, 3], lbv[:, 1], lbv[:, 2], ALU.add).then_inc(s_dve_chain, 1)
            dve.wait_ge(s_dve_chain, nth(dve, s_dve_chain))
            V.reciprocal(lbv[:, 4], lbv[:, 3]).then_inc(s_dve_chain, 1)
            dve.wait_ge(s_dve_chain, nth(dve, s_dve_chain))
            V.tensor_tensor(lbv[:, 1:3], lbv[:, 1:3], lbv[:, 4:5].broadcast_to([P, 2, HH]), ALU.mult).then_inc(s_dve_chain, 1)
            dve.wait_ge(s_dve_chain, nth(dve, s_dve_chain))
            V.tensor_tensor(lbv[:, 5], lbv[:, 1], lbv[:, 2], ALU.add).then_inc(s_dve_chain, 1)
            dve.wait_ge(s_dve_chain, nth(dve, s_dve_chain))
            V.tensor_tensor(lbv[:, 6], lbv[:, 1], lbv[:, 1], ALU.subtract).then_inc(s_dve_chain, 1)
            dve.wait_ge(s_dve_chain, nth(dve, s_dve_chain))
            V.tensor_tensor(lbv[:, 7], lbv[:, 5], lbv[:, 1], ALU.subtract).then_inc(s_dve_chain, 1)
            dve.wait_ge(s_dve_chain, nth(dve, s_dve_chain))
            V.tensor_scalar(lbv[:, 6:8], lbv[:, 6:8], -1.0, 1.0, ALU.mult, ALU.add).then_inc(s_dve_chain, 1)
            dve.wait_ge(s_dve_chain, nth(dve, s_dve_chain))

            for s, kind in enumerate(subs):
                modulation(s)
                if s < FIRST2:
                    by_rstd(x[:], xc[:])
                    affine(h, xc, mod[:, 8:16], mod[:, 0:8]).then_inc(s_h_ready, 1)
                else:
                    affine(h, x, mod[:, 8:16], mod[:, 0:8]).then_inc(s_h_ready, 1)
                    dve.wait_ge(s_h_ready, s + 1)
                    V.tensor_scalar(x[:], x[:], ALPHA, None, ALU.mult).then_inc(s_dve_chain, 1)
                    dve.wait_ge(s_dve_chain, nth(dve, s_dve_chain))
                if kind == "mla":
                    raw = rec[:, 8:16]
                    by_rstd(raw, raw)
                    affine(rec[:, 0:8], raw, modc[:, 8:16], modc[:, 0:8]).then_inc(s_context_ready, 1)
                    mla(s)
                    residual(s, "wo")
                if kind == "fourier":
                    residual(s, "wf")
                if kind == "ffn":
                    ffn = subs[:s].count("ffn")
                    u0 = unit0[s, "w13"]
                    for i, j in blocks(dve, by_name[s, "w13"]):
                        for c in range(2):
                            n = 2 * j + c
                            m = i * 2 * SLOTS + n
                            dst = big[:, m] if isinstance(m, int) else \
                                big[:, bass.ds(m, 1), :].rearrange("p a b -> p (a b)")
                            dve.wait_ge(s_silu, i * 2 * SLOTS + (ffn * KF + n + 1))
                            V.tensor_tensor(dst, sil[:, n % 2], lin[(u0 + n) % NBANK][:, T:2 * T],
                                            ALU.mult).then_inc(s_taken_by_dve, 1)
                    residual(s, "w2")
                if kind == "mix":
                    mix(s)
                    residual(s, "wout")
                if s < FIRST2:
                    dve.sem_inc(s_x_new, 1)
                else:
                    n = s - FIRST2
                    dve.sem_inc(s_x_summable, 1)
                    dve.wait_ge(s_mean_sums, nth(dve, s_mean_sums))
                    for k in range(0, KD, 4):
                        ps = pa[2][:, 0:T].unsqueeze(1).broadcast_to([P, 4, T])
                        V.scalar_tensor_tensor(xc[:, k:k + 4], ps, -1.0 / D, x[:, k:k + 4],
                                               ALU.mult, ALU.add).then_inc(s_x_centred, 1)
                    dve.wait_ge(s_x_centred, nth(dve, s_x_centred, 2))
                    by_rstd(xc[:], xc[:])
                    g, b = VC["ln_g"] + 8 * n, VC["ln_b"] + 8 * n
                    affine(x, xc, vec[:, g:g + 8], vec[:, b:b + 8]).then_inc(s_x_new, 1)
                dve.wait_ge(s_x_new, nth(dve, s_x_new))

        @block.tensor
        def _(pe):
            mm = nc.tensor.matmul

            def slot_of(ph, i, j):
                n = ph.first + j
                pe.wait_ge(s_weights[n % SLOTS], (i + (n // SLOTS + 1)) * 16)
                return ring[n % SLOTS]

            def bank(u, i=0, per=0):
                if isinstance(i, int):
                    u, i = u + i * per, 0
                    if u >= NBANK:
                        pe.wait_ge(*taken(u - NBANK))
                    return lin[u % NBANK]
                s, n = taken(u - NBANK)
                pe.wait_ge(s, i * per + n)
                return lin[u % NBANK]

            def tile_sum(dst, w, at, nk, rhs, m=P, step=None):
                for k in range(nk):
                    lo = at + k * (step or m)
                    ins = mm(dst, w[:, lo:lo + m], rhs(k), start=k == 0, stop=k == nk - 1)
                return ins

            def over_features(src, nk, dst):
                for k in range(nk):
                    ins = mm(dst, ones[:], src(k), start=k == 0, stop=k == nk - 1)
                return ins

            def squares_summed():
                pe.wait_ge(s_squares, nth(pe, s_squares, 1))
                for k in range(KD):
                    if k == 4:
                        pe.wait_ge(s_squares, nth(pe, s_squares, 1))
                    ins = mm(pstat[:, 0:T], ones[:], sq[:, k], start=k == 0, stop=k == KD - 1)
                ins.then_inc(s_sums_over_features, 1)

            def project(s, name, rhs):
                ph = by_name[s, name]
                nk = ph.cols // (ph.per * P)
                for i, j in blocks(pe, ph):
                    w = slot_of(ph, i, j)
                    for c in range(ph.per):
                        b = bank(ph.unit0 + j * ph.per + c, i, SLOTS * ph.per)
                        tile_sum(b[:, 0:T], w, c * nk * P, nk, rhs).then_inc(s_unit, 1)

            def pairs(ph, i, j, units, rhs):
                w = slot_of(ph, i, j)
                for c in range(units):
                    b = bank(ph.unit0 + j * ph.per + c, i, SLOTS * ph.per)
                    for g in range(2):
                        ins = tile_sum(b[:, g * T:(g + 1) * T], w, (2 * c + g) * KD * P, KD, rhs)
                    ins.then_inc(s_unit, 1)

            def turn(dst, src):
                return nc.tensor.transpose(dst, src, ident[:])

            def mla(s):
                hc = rec[:, 0:8]
                u = unit0[s, "in_a"]
                lat, con = (lambda k: h[:, k]), (lambda k: hc[:, k])
                w = slot_of(by_name[s, "in_a"], 0, 0)
                b = bank(u)
                tile_sum(b[:, 0:T], w, 0, KD, lat)
                tile_sum(b[:, T:2 * T], w, KD * P, KD, lat).then_inc(s_unit, 1)
                tile_sum(bank(u + 1)[:, 0:T], w, 2 * KD * P, KD, lat).then_inc(s_unit, 1)
                pe.wait_ge(s_context_ready, nth(pe, s_context_ready))
                b = bank(u + 2)
                tile_sum(b[:, 0:T], w, 3 * KD * P, KD, lat)
                tile_sum(b[:, T:2 * T], w, 3 * KD * P, KD, con).then_inc(s_unit, 1)
                w = slot_of(by_name[s, "in_b"], 0, 0)
                b = bank(u + 3)
                tile_sum(b[:, 0:T], w, 0, KD, lat)
                tile_sum(b[:, T:2 * T], w, 0, KD, con).then_inc(s_unit, 1)
                b = bank(u + 4)
                tile_sum(b[64:96, 0:T], w, KD * P, KD, lat, ROPE)
                tile_sum(b[64:96, T:2 * T], w, KD * P, KD, con, ROPE).then_inc(s_unit, 1)
                for j in range(3):
                    pairs(by_name[s, "in_c"], 0, j, 2, lat)
                pe.wait_ge(s_latent_squares, nth(pe, s_latent_squares))
                over_features(lambda k: sq[:, k], KQ, pstat[:, 0:T])
                kv_sq = sq[:, 3:7].rearrange("p (k t) c -> p k (t c)", t=2)
                over_features(lambda k: kv_sq[:, k], KKV, pa[0][:]).then_inc(s_latent_sums, 1)
                pe.wait_ge(s_latents_normed, nth(pe, s_latents_normed))
                cq, ckv = proj[:, 12:15], proj[:, 15:19].rearrange("p (k t) c -> p k (t c)", t=2)
                w = slot_of(by_name[s, "uq"], 0, 0)
                for n in range(4):
                    b = bank(u + 11 + n)
                    for c in range(2):
                        ins = tile_sum(b[0:QKD, c * T:(c + 1) * T], w, (2 * n + c) * QKD, KQ, lambda k: cq[:, k], QKD,
                                       MLA_H * QKD)
                    ins.then_inc(s_unit, 1)
                w = slot_of(by_name[s, "ukv"], 0, 0)
                for n in range(MLA_H):
                    b = bank(u + 15 + n)
                    tile_sum(b[0:NOPE], w, n * NOPE, KKV, lambda k: ckv[:, k], NOPE, MLA_H * NOPE).then_inc(s_unit, 1)
                for n in range(4):
                    b = bank(u + 23 + n)
                    for k in range(KKV):
                        ins = mm(b[:], ckv[:, k, n * P:(n + 1) * P], w[:, 1024 + k * 512:1536 + k * 512],
                                 start=k == 0, stop=k == KKV - 1)
                    ins.then_inc(s_unit, 1)
                qh = big[0:QKD, 16:24].rearrange("p (h t) c -> p h (t c)", t=2)
                kh = big[:, 0:16].rearrange("p (h t) c -> p h (t c)", t=2)
                pe.wait_ge(s_head_squares, nth(pe, s_head_squares))
                for n in range(12):
                    src = sq[0:QKD, 2 * n:2 * n + 2] if n < 4 else rec[0:QKD, 2 * n - 8:2 * n - 6]
                    if n >= 4:
                        pe.wait_ge(s_head_deviation, nth(pe, s_head_deviation))
                    mm(pa[n % 4][0:QKD], ones[0:QKD, 0:QKD], src.rearrange("p a b -> p (a b)"),
                       start=True, stop=True).then_inc(s_head_sum, 1)
                pe.wait_ge(s_head_deviation, nth(pe, s_head_deviation, 4))
                rot = bias[0:QKD, 1, 0, 0:QKD]
                pe.wait_ge(s_head_normed, nth(pe, s_head_normed, 12))
                for n in range(8):
                    if n >= 4:
                        pe.wait_ge(s_rotated, nth(pe, s_rotated))
                    src = qh[:, n] if n < 4 else big[0:QKD, 4 * (n - 4):4 * (n - 4) + 3:2]
                    dst = pa[n % 4][0:QKD] if n < 4 else pa[n % 4][0:QKD].rearrange("p (a b) -> p a b", a=2)
                    mm(dst, rot, src, start=True, stop=True).then_inc(s_half_turned, 1)
                pe.wait_ge(s_rotated, nth(pe, s_rotated, 4))

                def logits(n):
                    a, tt = n // 2, n % 2
                    q = big[0:QKD, 16 + a, tt * P:tt * P + P]
                    mm(pa[n % 2][:], q, kh[0:QKD, a], start=True, stop=True).then_inc(s_logits, 1)

                def attend(n):
                    a, tt = n // 2, n % 2
                    pe.wait_ge(s_p_turned_taken, nth(pe, s_p_turned_taken))
                    if n % 4 == 0 and n >= 8:
                        pe.wait_ge(s_head_pair_taken, nth(pe, s_head_pair_taken))
                    lo = (a % 2) * VD
                    dst = (pa[3], pstat)[n // 4 % 2][lo:lo + VD, tt * P:tt * P + P]
                    vt = tok[:].rearrange("p a (b c) -> p (a b) c", c=512)
                    pt = sq[:, 4 + 2 * (n % 2):6 + 2 * (n % 2)].rearrange("p a (b c) -> p (a b) c", b=2)
                    for k in range(4):
                        ins = mm(dst, vt[:, k, a * VD:(a + 1) * VD], pt[:, k], start=k == 0, stop=k == 3)
                    if n % 4 == 3:
                        ins.then_inc(s_head_pair, 1)

                logits(0)
                for n in range(2 * MLA_H):
                    if n + 1 < 2 * MLA_H:
                        logits(n + 1)
                    pe.wait_ge(s_p_normed, nth(pe, s_p_normed))
                    if n:
                        attend(n - 1)
                    p = sq[:, 2 * (n % 2):2 * (n % 2) + 2].rearrange("p a (b c) -> p (a b) c", b=2)
                    for k in range(4):
                        ins = turn(pa[2][:, k * P:(k + 1) * P], p[:, k])
                    ins.then_inc(s_p_turned, 1)
                attend(2 * MLA_H - 1)
                pe.wait_ge(s_head_pair_taken, nth(pe, s_head_pair_taken, 2))
                pe.wait_ge(s_conv_done, nth(pe, s_conv_done))

            def fourier(s):
                u, ph = unit0[s, "dft"], by_name[s, "dft"]
                w = slot_of(ph, 0, 0)
                dft_d = w[:, 0:1024].rearrange("p (k n) -> p k n", k=2)
                dft_t = w[:, 1024:2048].rearrange("p (k c n) -> p k c n", k=2, c=2)
                fa = big[:, 0:16].rearrange("p (u a) b -> p u (a b)", a=2)
                for g in range(4):
                    for tt in range(TT):
                        b = bank(u + 2 * g + tt)
                        for k in range(2):
                            ins = mm(b[:], h[:, 2 * g + k, tt * P:tt * P + P], dft_d[:, k], start=k == 0, stop=k == 1)
                        ins.then_inc(s_unit, 1)
                pe.wait_ge(*taken(u + 7))
                for g in range(4):
                    b = bank(u + 8 + g)
                    for j in range(2):
                        for n, (tt, c) in enumerate(((0, 0), (0, 1), (1, 0), (1, 1))):
                            ins = mm(b[:, j * T:(j + 1) * T], fa[:, 2 * g + tt, c * T + j * P:c * T + j * P + P],
                                     dft_t[:, tt, c], start=n == 0, stop=n == 3)
                    ins.then_inc(s_unit, 1)
                pe.wait_ge(*taken(u + 11))

            def mix(s):
                l = subs[:s].count("mix")
                rhs = lambda k: h[:, k]
                u = unit0[s, "mproj"]
                for n in range(5):
                    pairs(by_name[s, "mproj"], n // SLOTS, n % SLOTS, 2, rhs)
                w = slot_of(by_name[s, "mlast"], 0, 0)
                b = bank(u + 10)
                tile_sum(b[:, 0:T], w, 0, KD, rhs)
                for tt in range(TT):
                    for k in range(KD):
                        ins = mm(b[:, T + tt * IH:T + (tt + 1) * IH], h[:, k, tt * P:tt * P + P],
                                 w[:, 1024 + k * IH:1024 + (k + 1) * IH], start=k == 0, stop=k == KD - 1)
                ins.then_inc(s_unit, 1)
                for n in range(4):
                    if n % 2 == 0:
                        w = slot_of(by_name[s, "mtok"], 0, n // 2)
                    b = bank(u + 11 + n)
                    tt = n % 2
                    for k in range(KD):
                        ins = mm(b[:], h[:, k, tt * P:tt * P + P], w[:, k * 512:(k + 1) * 512],
                                 start=k == 0, stop=k == KD - 1)
                    ins.then_inc(s_unit, 1)
                w = slot_of(by_name[s, "pool"], 0, 0)
                b = bank(u + 15)
                pe.wait_ge(*taken(u + 12))
                for g in range(4):
                    lo = (g % 2) * 64
                    for k in range(TT):
                        ins = mm(b[lo:lo + 64, (g // 2) * T:(g // 2 + 1) * T], tok[:, k, g * 64:(g + 1) * 64],
                                 w[:, (g * TT + k) * T:(g * TT + k + 1) * T], start=k == 0, stop=k == TT - 1)
                ins.then_inc(s_unit, 1)
                pe.wait_ge(*taken(u + 10))
                for n in range(TT * IH // 2):
                    if n >= 4:
                        pe.wait_ge(s_index_relu, nth(pe, s_index_relu))
                    tt, pair, lo = n // 4, n % 4 // 2, (n % 2) * 64
                    for c in range(2):
                        ins = mm(pa[n % 4][:, c * T:(c + 1) * T],
                                 proj[lo:lo + 64, QI + 2 * pair + c, tt * P:tt * P + P],
                                 proj[lo:lo + 64, KI], start=True, stop=True)
                    ins.then_inc(s_index_products, 1)
                pe.wait_ge(s_index_relu, nth(pe, s_index_relu, 4))
                pe.wait_ge(*taken(u + 15))
                b = bank(u + 16)
                for g in range(4):
                    lo = (g % 2) * 64
                    ins = mm(b[lo:lo + 64, (g // 2) * T:(g // 2 + 1) * T], poolw[lo:lo + 64, l, g // 2],
                             work[lo:lo + 64, g // 2], start=True, stop=True)
                ins.then_inc(s_unit, 1)

                ph = by_name[s, "gates"]
                g = [0]

                def gate_units(n):
                    for _ in range(n):
                        m = g[0]
                        g[0] += 1
                        if m % 2 == 0:
                            gw[0] = slot_of(ph, m // 2 // SLOTS, m // 2 % SLOTS)
                        b = bank(ph.unit0 + m)
                        for c in range(2):
                            ins = tile_sum(b[:, c * T:(c + 1) * T], gw[0], (2 * (m % 2) + c) * KD * P, KD, rhs)
                        ins.then_inc(s_unit, 1)

                gw = [None]
                q_l, k_l = rec[:, 8:12], rec[:, 12:16]
                gate_units(GATES_AT[0])
                pe.wait_ge(s_level_ready, nth(pe, s_level_ready))
                for a in range(HH):
                    ins = mm(pa[0][:, a * P:(a + 1) * P], k_l[:, a, 0:P], q_l[:, a, P:2 * P], start=True, stop=True)
                ins.then_inc(s_level_products, 1)
                pe.wait_ge(s_level_products, nth(pe, s_level_products))
                pe.sem_inc(s_far_summed, 1)
                for n in range(1, 7):
                    pe.wait_ge(s_level_ready, nth(pe, s_level_ready))
                    if n == 2:
                        pe.wait_ge(s_far_scores, nth(pe, s_far_scores))
                    if n >= 3:
                        pe.wait_ge(s_level_added, nth(pe, s_level_added, 2))
                    for tt in range(TT):
                        for a in range(HH):
                            ins = mm(pa[2 * (n % 2) + tt][:, a * P:(a + 1) * P], k_l[:, a, tt * P:tt * P + P],
                                     q_l[:, a, tt * P:tt * P + P], start=True, stop=True)
                        if tt == 0:
                            ins.then_inc(s_level_scores, 1)
                    ins.then_inc(s_level_products, 1)
                    pe.wait_ge(s_level_products, nth(pe, s_level_products))
                    pe.sem_inc(s_level_scores, 1)
                    gate_units(GATES_AT[n])
                pe.wait_ge(s_level_added, nth(pe, s_level_added, 4))
                for tt in range(TT):
                    for half in range(2):
                        lo = half * 64
                        for c in range(2):
                            ins = mm(pa[2 * tt + half][:, c * T:(c + 1) * T],
                                     proj[lo:lo + 64, AQ + c, tt * P:tt * P + P], proj[lo:lo + 64, AK + c],
                                     start=True, stop=True)
                        ins.then_inc(s_attention_logits, 1)
                for tt in range(TT):
                    pe.wait_ge(s_weights_ready, nth(pe, s_weights_ready))
                    for kt in range(TT):
                        for a in range(AH):
                            ins = turn(pa[2 * tt + kt][:, a * P:(a + 1) * P], att[:, a, kt * P:kt * P + P])
                    ins.then_inc(s_weights_turned, 1)
                    pe.wait_ge(s_weights_turned_taken, nth(pe, s_weights_turned_taken))
                    if tt:
                        pe.wait_ge(s_attended_taken, nth(pe, s_attended_taken))
                    for place, a in enumerate(HEAD_ORDER):
                        lo = (a % 2) * 64
                        for kt in range(TT):
                            pt = att[:, 4 + 2 * kt + place // 2, (place % 2) * P:(place % 2) * P + P]
                            ins = mm(pstat[lo:lo + 64, (a // 2) * P:(a // 2 + 1) * P],
                                     tok[:, kt, 256 + a * 64:320 + a * 64], pt, start=kt == 0, stop=kt == TT - 1)
                    ins.then_inc(s_attended, 1)
                    gate_units(GATES_AT[7 + tt])
                for tt in range(TT):
                    for a in range(HH):
                        dst = pa[tt][:, a * P:(a + 1) * P]
                        near = sq[:, 2 * tt + a // 2, (a % 2) * P:(a % 2) * P + P]
                        ins = mm(dst, tok[:, tt, 512 + a * P:512 + (a + 1) * P], near, start=True, stop=tt == 0)
                        if tt:
                            far = sq[:, 4 + a // 2, (a % 2) * P:(a % 2) * P + P]
                            ins = mm(dst, tok[:, 0, 512 + a * P:512 + (a + 1) * P], far, start=False, stop=True)
                    ins.then_inc(s_recurrence_out, 1)
                pe.wait_ge(s_recurrence_squares, nth(pe, s_recurrence_squares))
                for n in range(2):
                    mm(pa[2 + n][:], ones[:], rec[:, 4 + 2 * n:6 + 2 * n].rearrange(
                        "p a b -> p (a b)"), start=True, stop=True).then_inc(s_recurrence_sums, 1)
                gate_units(12 - g[0])
                pe.wait_ge(s_recurrence_ready, nth(pe, s_recurrence_ready))
                pe.wait_ge(s_attended_taken, nth(pe, s_attended_taken))
                pe.wait_ge(*taken(u + 16))
                ph = by_name[s, "branch"]
                for m in range(KD):
                    if m % 4 == 0:
                        w = slot_of(ph, 0, m // 4)
                    at = (m % 4) * KD * P
                    b = bank(ph.unit0 + 2 * m)
                    tile_sum(b[:, 0:T], w, at, 2, lambda k: yab[:, k])
                    tile_sum(b[:, T:2 * T], w, at + 2 * P, 2, lambda k: yab[:, 2 + k]).then_inc(s_unit, 1)
                    b = bank(ph.unit0 + 2 * m + 1)
                    tile_sum(b[:, 0:T], w, at + 4 * P, 4, lambda k: rec[:, k]).then_inc(s_unit, 1)
                pe.wait_ge(s_branches_merged, nth(pe, s_branches_merged, KD))


            pe.wait_ge(s_tables_dma, nth(pe, s_tables_dma, 10))
            for a in range(AH):
                rb = work[0:BUCKETS].rearrange("p a b -> p (a b)")[:, a * P:(a + 1) * P]
                mm(pa[a][:], rb, sil[0:BUCKETS].rearrange("p a b -> p (a b)"),
                   start=True, stop=True).then_inc(s_bias_row_summed, 1)
            pe.wait_ge(s_fills, nth(pe, s_fills, 3))
            pe.wait_ge(s_bias_rows_dma, nth(pe, s_bias_rows_dma, AH))

            for s, kind in enumerate(subs):
                if s < FIRST2:
                    squares_summed()
                if kind == "mla":
                    squares_summed()
                pe.wait_ge(s_ada_ready, nth(pe, s_ada_ready))
                if s == 0:
                    for m in range(16):
                        mm(pa[3][:, 32 + m:33 + m], big[:, m // 2, (m % 2) * P:(m % 2) * P + P], ones[:, 0:1],
                           start=True, stop=True)
                for m in range(24):
                    ins = mm(pa[3][:, m:m + 1], ada_sum[:, m * P:(m + 1) * P], ones[:, 0:1], start=True, stop=True)
                ins.then_inc(s_modulation_summed, 1)
                pe.wait_ge(s_h_ready, nth(pe, s_h_ready))
                if kind == "mla":
                    mla(s)
                    project(s, "wo", lambda k: h[:, k])
                if kind == "fourier":
                    fourier(s)
                    project(s, "wf", lambda k: h[:, k])
                if kind == "ffn":
                    ph = by_name[s, "w13"]
                    for i, j in blocks(pe, ph):
                        pairs(ph, i, j, 2, lambda k: h[:, k])
                    pe.wait_ge(*taken(unit0[s, "w2"] - 1))
                    project(s, "w2", lambda k: big[:, k])
                if kind == "mix":
                    mix(s)
                    project(s, "wout", lambda k: h[:, k])
                if s >= FIRST2:
                    pe.wait_ge(s_x_summable, nth(pe, s_x_summable))
                    over_features(lambda k: x[:, k], KD, pa[2][:, 0:T]).then_inc(s_mean_sums, 1)
                    squares_summed()



def tables():
    f = np.float32
    t = np.arange(T)
    out = {}
    inv = 1.0 / (10000.0 ** (np.arange(0, ROPE // 2, 2) / (ROPE // 2)))
    rope = np.zeros((QKD, 2, T))
    for half, pos in enumerate((t // 64, t % 64)):
        ang = (pos[None, :].astype(f) * inv[:, None].astype(f)).astype(f)
        for part in range(2):
            lo = NOPE + 16 * half + 8 * part
            rope[lo:lo + 8, 0], rope[lo:lo + 8, 1] = np.cos(ang), np.sin(ang)
    out["rope"] = rope.astype(f)
    rot = np.zeros((QKD, QKD), f)
    for half in range(2):
        for i in range(8):
            a = NOPE + 16 * half + i
            rot[a + 8, a], rot[a, a + 8] = -1.0, 1.0
    out["rot"] = rot
    out["ident"] = np.eye(P, dtype=f)
    ang = 2 * np.pi * (np.outer(t, t) % T) / T
    cs = np.concatenate([np.cos(ang), np.sin(ang)], 1).reshape(2, P, 512).transpose(1, 0, 2).reshape(P, 1024)
    ct = np.stack([np.cos(ang), -np.sin(ang)], 1).reshape(2, P, 512).transpose(1, 0, 2).reshape(P, 1024) / T
    out["dft"] = np.concatenate([cs, ct], 1).astype(f)[None]
    i = np.arange(P)
    S, U = i[:, None], i[None, :]
    lv = [(S // (2 * m) == U // (2 * m)) & (S % (2 * m) < m) & (U % (2 * m) >= m) for m in LEVELS]
    lv.append((S // 4 == U // 4) & (S <= U))
    out["masks"] = np.stack(lv, 1).astype(f)
    out["causal"] = (t[None, :] <= t[:, None]).reshape(TT, P, T).transpose(1, 0, 2).astype(f)
    pm = np.zeros((T, 4, T))
    for g, w in enumerate((2, 4, 8, 16)):
        for q in range(T):
            pm[max(0, q - w + 1):q + 1, g, q] = 1.0 / min(q + 1, w)
            pm[q, g, q] -= 1.0
    out["poolm"] = pm.reshape(TT, P, 4, T).transpose(1, 2, 0, 3).reshape(1, P, 2048).astype(f)
    dist = np.maximum(255 - np.arange(512), 0)
    exact = BUCKETS // 2
    large = exact + (np.log(np.maximum(dist, 1).astype(f) / f(exact)) / f(np.log(MAX_DIST / exact))
                     * f(BUCKETS - exact)).astype(np.int32)
    bucket = np.where(dist < exact, dist, np.minimum(large, BUCKETS - 1))
    out["onehot"] = (bucket[None, :] == np.arange(BUCKETS)[:, None]).astype(f).reshape(BUCKETS, 2, T)
    return {k: np.ascontiguousarray(v, dtype=f) for k, v in out.items()}



def feature_major(v):
    v = np.asarray(v)
    if v.ndim == 1:
        return v.reshape(-1, P).T
    return v.T.reshape(-1, P, v.shape[0]).transpose(1, 0, 2)


def blocks_of(w, per):
    k, n = w.shape
    return w.reshape(k // P, P, n // (P * per), per, P).transpose(2, 1, 3, 0, 4).reshape(n // (P * per), P, -1)


def rows_in(w):
    return w.reshape(-1, P, w.shape[1]).transpose(1, 0, 2).reshape(P, -1)


def gate_up(a, b):
    k, n = a.shape
    w = np.stack([a.reshape(k, n // P, P), b.reshape(k, n // P, P)], 2).reshape(k, 2 * n)
    return blocks_of(w, 4)


def layout(v):
    L = tables()
    L["x"] = feature_major(v["x"][0])
    L["ctx"] = feature_major(v["ctx"][0])
    L["cols"] = np.stack([feature_major(v["c"][0]), feature_major(v["c_ctx"]), feature_major(v["c_2"][0])], 1)
    ada = np.concatenate([v["ada_w"].reshape(DEPTH, D, 2, MODC).transpose(0, 2, 1, 3).reshape(4, D, MODC),
                          v["w_ada_2"].reshape(DEPTH, D, 3, MODC).transpose(0, 2, 1, 3).reshape(6, D, MODC)])
    L["ada"] = ada.reshape(10, KD, P, ADA_N, ADA_C).transpose(0, 3, 2, 1, 4).reshape(10 * ADA_N, P, KD, ADA_C)
    L["ada_b"] = np.concatenate([v["ada_b"].reshape(4, 24, P), v["b_ada_2"].reshape(6, 24, P)]).transpose(2, 0, 1)
    gains = np.zeros((2, P), np.float32)
    gains[0, :QKD], gains[1, :QKD] = v["q_gain"][0], v["k_gain"][0]
    norm_g = np.stack([v["norm1_g"], v["norm2_g"]], 1)
    L["vec"] = np.concatenate([norm_g.reshape(-1, P), v["q_norm_g"].reshape(-1, P), v["kv_norm_g"].reshape(-1, P),
                               gains, v["conv_w"][0].reshape(-1, P), v["ln_g_2"].reshape(-1, P),
                               v["ln_b_2"].reshape(-1, P), v["pool_scale_2"].reshape(-1, P),
                               v["hgrn_lb_2"].reshape(-1, P), v["hgrn_norm_g_2"].reshape(-1, P)]).T
    L["poolw"] = v["pool_w_2"].reshape(DEPTH, 2, 2, 64, 64).transpose(2, 3, 0, 1, 4).reshape(P, DEPTH, 2, 64)
    rb = v["rel_bias_2"]
    L["relb"] = np.broadcast_to(rb[:, :, None], (BUCKETS, AH, P)).reshape(BUCKETS, 2, T)
    w = v["w_in"][0]
    at = QL + KVL
    L["w_in_a"] = blocks_of(w[:, 0:512], 4)
    L["w_in_b"] = np.concatenate([rows_in(w[:, 512:at]), rows_in(w[:, at:at + ROPE])], 1)[None]
    L["w_in_c"] = blocks_of(w[:, at + ROPE:], 4)
    L["w_uq"] = rows_in(v["w_uq"][0])[None]
    kv = v["w_ukv"][0].reshape(KVL, MLA_H, NOPE + VD)
    L["w_ukv"] = np.concatenate([rows_in(kv[:, :, :NOPE].reshape(KVL, -1)), rows_in(kv[:, :, NOPE:].reshape(KVL, -1))],
                                1)[None]
    L["w_o"] = blocks_of(v["w_o"][0], 4)
    L["w_f"] = blocks_of(v["w_fourier"][0], 4)
    w13 = [gate_up(v["ffn_w1"][i], v["ffn_w3"][i]) for i in range(DEPTH)]
    w2 = [blocks_of(v["ffn_w2"][i], 1) for i in range(DEPTH)]
    mproj, mlast, mtok, gates = [], [], [], []
    for l in range(DEPTH):
        for j in range(2):
            w = v["ffn_w_in_2"][l, j]
            w13.append(gate_up(w[:, :FF], w[:, FF:]))
            w2.append(blocks_of(v["ffn_w_out_2"][l, j], 1))
        w = v["mix_w_in_2"][l]
        a, q, k, val, qi, ki, wi, hq, hf, hi, hg, gt = np.split(
            w, np.cumsum([256, 256, 256, 256, 512, 64, 8, 512, 512, 512, 512]), axis=1)
        tiles = np.concatenate([hf, hq, qi, ki, ki, q, k, hg], 1)
        mproj.append(blocks_of(tiles[:, :20 * P], 4))
        mlast.append(np.concatenate([rows_in(tiles[:, 20 * P:]), rows_in(wi)], 1)[None])
        mtok.append(np.stack([rows_in(np.concatenate([a, val], 1)), rows_in(hi)]))
        gates.append(blocks_of(gt, 4))
    L["w13"], L["w2"] = np.stack(w13), np.stack(w2)
    L["mproj"], L["mlast"], L["mtok"], L["gates"] = map(np.stack, (mproj, mlast, mtok, gates))
    L["branch"] = np.stack([blocks_of(w, 4) for w in v["w_branch_2"]])
    L["wout"] = np.stack([blocks_of(w, 4) for w in v["w_out_2"]])
    return {k: np.ascontiguousarray(a) for k, a in L.items()}


def kernel(**inputs):
    import concourse.bacc as bacc
    from concourse.bass_utils import run_bass_kernel_spmd

    nc = bacc.Bacc("TRN2", target_bir_lowering=False, num_devices=1)
    laid = layout({k: np.asarray(a) for k, a in inputs.items()})
    I = {k: nc.dram_tensor(f"in_{k}", a.shape, mybir.dt.from_np(a.dtype), kind="ExternalInput").ap()
         for k, a in laid.items()}
    out = nc.dram_tensor("out", (P, KD, T), F32, kind="ExternalOutput").ap()
    build(nc, I, out)
    r = run_bass_kernel_spmd(nc, [{f"in_{k}": a for k, a in laid.items()}], core_ids=[0])
    y = r.results[0]["out"]
    return np.ascontiguousarray(y.transpose(1, 0, 2).reshape(D, T).T[None])
```

```python
from contextlib import ExitStack

import numpy as np
import concourse.bass as bass
from concourse import mybir

ALU = mybir.AluOpType
ACT = mybir.ActivationFunctionType
F32 = mybir.dt.float32
AX = mybir.AxisListType.X

P = 128
T = 256
D = 1024
KD = D // P
TT = T // P
FF = 2816
KF = FF // P
DEPTH = 2

MLA_H, NOPE, ROPE, VD = 8, 64, 32, 64
QKD = NOPE + ROPE
QL, KVL = 384, 256
KQ, KKV = QL // P, KVL // P
CONV = 512
KC = CONV // P
QK_SCALE = QKD ** -0.5

AH, IH = 4, 8
TOPK = 64
BUCKETS, MAX_DIST = 32, 128
HH = 4
KEY_MAX = float(np.float32(1.0 - 1e-6))
ALPHA = (2 * DEPTH) ** 0.25
IDX_SCALE = (64 ** -0.5) * (IH ** -0.5)
AT_SCALE = 64 ** -0.5
TAKEN, UNSEEN = -3.3e38, -3.0e38

SUBS = ["mla", "ffn", "fourier", "ffn", "ffn", "mix", "ffn", "ffn", "mix", "ffn"]
FIRST2 = 4
MODC = 3 * D
ADA_C = 128
ADA_N = MODC // ADA_C
FIRST_N = 2 * D // (2 * P)
BY_PE = (0, 3, 6)
FIRST_GATE = 2 * D // ADA_C

SLOTS = 3
SLOT = 4096
NBANK = 3

HF, HQ, QI, KI, AQ, AK, HG = 0, 4, 8, 12, 13, 15, 17
NPROJ = 21
LEVELS = [64, 32, 16, 8, 4]


HEAD_ORDER = [0, 2, 1, 3]
GATES_AT = [3, 1, 1, 1, 1, 1, 1, 1, 1]

VC, NVEC = {}, 0
for _name, _n in (("norm_g", 32), ("q_norm", 3), ("kv_norm", 2), ("q_gain", 2), ("conv", 12), ("ln_g", 48),
                  ("ln_b", 48), ("pool_scale", 4), ("lb", 8), ("hgrn_norm", 8)):
    VC[_name] = NVEC
    NVEC += _n


FIRST_PHASE = {"mla": "in_a", "ffn": "w13", "fourier": "dft", "mix": "mproj"}


class Phase:

    def __init__(self, name, src, nb, cols, first, unit0, per):
        self.name, self.src, self.nb, self.cols, self.first = name, src, nb, cols, first
        self.unit0, self.per = unit0, per


def build(nc, I, out, stop=10, dbg=None):
    subs = SUBS[:stop]
    with ExitStack() as ctx:
        def sb(name, shape):
            return ctx.enter_context(nc.sbuf_tensor(name, shape, F32))

        def sem(name):
            return ctx.enter_context(nc.semaphore(name))

        ring = [sb(f"ring{i}", [P, SLOT]) for i in range(SLOTS)]
        ada_ring = [sb(f"ada_ring{i}", [P, KD, ADA_C]) for i in range(2)]
        ada_sum = sb("ada_sum", [P, MODC])
        x = sb("x", [P, KD, T])
        xc = sb("xc", [P, KD, T])
        sq = sb("sq", [P, KD, T])
        h = sb("h", [P, KD, T])
        big = sb("big", [P, 24, T])
        proj = sb("proj", [P, 24, T])
        rec = sb("rec", [P, 16, T])
        tok = sb("tok", [P, TT, 1024])
        att = sb("att", [P, 8, T])
        yab = sb("yab", [P, 4, T])
        sil = sb("sil", [P, 2, T])
        sd = sb("sd", [P, T])
        rstd = sb("rstd", [P, T])
        bias = sb("bias", [P, AH, TT, T])
        cols = sb("cols", [P, 3, KD])
        csil = sb("csil", [P, 3, KD])
        ada_b = sb("ada_b", [P, 10, 24])
        mod = sb("mod", [P, 24])
        modc = sb("modc", [P, 16])
        vec = sb("vec", [P, NVEC])
        small = sb("small", [P, 64])
        lbv = sb("lbv", [P, 8, HH])
        ones = sb("ones", [P, P])
        eps = sb("eps", [P, 2])
        ident = sb("ident", [P, P])
        masks = sb("masks", [P, 6, P])
        causal = sb("causal", [P, TT, T])
        poolw = sb("poolw", [P, DEPTH, 2, 64])
        work = sb("work", [P, 2, T])
        top8 = sb("top8", [P, 16])

        lin = [ctx.enter_context(nc.psum_tensor(f"lin{i}", [P, 512], F32)) for i in range(NBANK)]
        pstat = ctx.enter_context(nc.psum_tensor("pstat", [P, 512], F32))
        pa = [ctx.enter_context(nc.psum_tensor(f"small_ps{i}", [P, 512], F32)) for i in range(4)]
        bias_rows = nc.dram_tensor("bias_rows", [AH, P * 512 + 512], F32, kind="Internal").ap()

        s_weights = [sem(f"weights_in_slot{i}") for i in range(SLOTS)]
        s_ada_dma = [sem(f"ada_weights_in_slot{i}") for i in range(2)]
        s_unit = sem("units_summed")
        s_taken_by_act, s_taken_by_dve = sem("units_taken_by_act"), sem("units_taken_by_dve")
        s_act_chain = sem("act_chain")
        s_ada_first_dma = [sem(f"first_ada_weights_in_slot{i}") for i in range(FIRST_N)]
        s_first_products = sem("first_products")
        s_first_summed = sem("first_modulation_summed")
        s_modulation_kept = sem("modulation_kept")
        s_bias_row_taken = sem("bias_row_taken")
        s_ada_ready = sem("ada_ready")
        s_attended = sem("attended")
        s_attended_taken = sem("attended_taken")
        s_attention_logits = sem("attention_logits")
        s_bias_dma = sem("bias_dma")
        s_bias_row_summed = sem("bias_row_summed")
        s_bias_rows_dma = sem("bias_rows_dma")
        s_bound_exps = sem("bound_exps")
        s_bound_logits = sem("bound_logits")
        s_branches_merged = sem("branches_merged")
        s_cols_dma = sem("cols_dma")
        s_context_ready = sem("context_ready")
        s_conv_done = sem("conv_done")
        s_ctx_dma = sem("ctx_dma")
        s_deviation = sem("deviation")
        s_dve_chain = sem("dve_chain")
        s_exponents = sem("exponents")
        s_far_scores = sem("far_scores")
        s_far_summed = sem("far_summed")
        s_fills = sem("fills")
        s_h_ready = sem("h_ready")
        s_half_turned = sem("half_turned")
        s_head_deviation = sem("head_deviation")
        s_head_normed = sem("head_normed")
        s_head_pair = sem("head_pair")
        s_head_pair_taken = sem("head_pair_taken")
        s_head_squares = sem("head_squares")
        s_head_sum = sem("head_sum")
        s_index_products = sem("index_products")
        s_index_relu = sem("index_relu")
        s_index_relu_used = sem("index_relu_used")
        s_k_rope_part = sem("k_rope_part")
        s_key_capped = sem("key_capped")
        s_latent_deviation = sem("latent_deviation")
        s_latent_squares = sem("latent_squares")
        s_latent_sums = sem("latent_sums")
        s_latents_normed = sem("latents_normed")
        s_level_added = sem("level_added")
        s_level_exps = sem("level_exps")
        s_level_products = sem("level_products")
        s_level_ready = sem("level_ready")
        s_level_scores = sem("level_scores")
        s_log_forget = sem("log_forget")
        s_logits = sem("logits")
        s_logits_exp = sem("logits_exp")
        s_logits_max = sem("logits_max")
        s_mean_sums = sem("mean_sums")
        s_modulation_ready = sem("modulation_ready")
        s_modulation_summed = sem("modulation_summed")
        s_p_normed = sem("p_normed")
        s_p_turned = sem("p_turned")
        s_p_turned_taken = sem("p_turned_taken")
        s_pool_chain = sem("pool_chain")
        s_recurrence_deviation = sem("recurrence_deviation")
        s_recurrence_out = sem("recurrence_out")
        s_recurrence_ready = sem("recurrence_ready")
        s_recurrence_squares = sem("recurrence_squares")
        s_recurrence_sums = sem("recurrence_sums")
        s_result_dma = sem("result_dma")
        s_rope_tables_used = sem("rope_tables_used")
        s_rotated = sem("rotated")
        s_row_exp = sem("row_exp")
        s_row_max = sem("row_max")
        s_rstd_made = sem("rstd_made")
        s_sigmoid_z = sem("sigmoid_z")
        s_silu = sem("silu")
        s_silu_c = sem("silu_c")
        s_silu_q_and_out_gate = sem("silu_q_and_out_gate")
        s_squares = sem("squares")
        s_sums_over_features = sem("sums_over_features")
        s_tables_dma = sem("tables_dma")
        s_mixer_tables_dma = sem("mixer_tables_dma")
        s_weights_ready = sem("weights_ready")
        s_weights_turned = sem("weights_turned")
        s_weights_turned_taken = sem("weights_turned_taken")
        s_x_centred = sem("x_centred")
        s_x_dma = sem("x_dma")
        s_x_new = sem("x_new")
        s_x_scaled = sem("x_scaled")

        followed = {}

        def nth(eng, s, times=1):
            key = (str(eng.engine), s.num)
            followed[key] = followed.get(key, 0) + times * (16 if s.num in by_dma else 1)
            return followed[key]

        by_dma = {x.num for x in (s_bias_dma, s_bias_rows_dma, s_cols_dma, s_ctx_dma, s_result_dma, s_tables_dma, s_x_dma)}

        phases, takes, unit0, unit_end = [], [], {}, []
        count = {"a": 0, "d": 0}

        def phase(s, name, src, nb, width, units, taker):
            first = phases[-1].first + phases[-1].nb if phases else 0
            phases.append(Phase((s, name), src, nb, width, first, len(takes), units // nb))
            unit_end.extend(len(takes) + (b + 1) * (units // nb) for b in range(nb))
            unit0[s, name] = len(takes)
            for _ in range(units):
                count[taker] += 1
                takes.append((taker, count[taker]))

        nf = nm = 0
        for s, kind in enumerate(subs):
            if kind == "mla":
                phase(s, "in_a", I["w_in_a"], 1, 4096, 3, "a")
                phase(s, "in_b", I["w_in_b"], 1, 1280, 2, "a")
                phase(s, "in_c", I["w_in_c"], 3, 4096, 6, "a")
                phase(s, "uq", I["w_uq"], 1, KQ * MLA_H * QKD, 4, "a")
                phase(s, "ukv", I["w_ukv"], 1, 2048, 12, "a")
                phase(s, "wo", I["w_o"], 2, 4096, 8, "d")
            elif kind == "fourier":
                phase(s, "dft", I["dft"], 1, 2048, 12, "a")
                phase(s, "wf", I["w_f"], 2, 4096, 8, "d")
            elif kind == "ffn":
                phase(s, "w13", I["w13"][nf], KF // 2, 4096, KF, "d")
                phase(s, "w2", I["w2"][nf], KD, FF, KD, "d")
                nf += 1
            else:
                phase(s, "mproj", I["mproj"][nm], 5, 4096, 10, "a")
                phase(s, "mlast", I["mlast"][nm], 1, 1088, 1, "a")
                phase(s, "mtok", I["mtok"][nm], 2, 4096, 4, "a")
                phase(s, "pool", I["poolm"], 1, 2048, 2, "a")
                phase(s, "gates", I["gates"][nm], 6, 4096, 12, "a")
                phase(s, "branch", I["branch"][nm], 2, 4096, 16, "d")
                phase(s, "wout", I["wout"][nm], 2, 4096, 8, "d")
                nm += 1
        by_name = {ph.name: ph for ph in phases}

        def blocks(eng, ph):
            whole = ph.nb // SLOTS if ph.nb >= 2 * SLOTS else 0
            if whole:
                with eng.Fori(0, whole) as i:
                    for j in range(SLOTS):
                        yield i, j
            for b in range(whole * SLOTS, ph.nb):
                yield b // SLOTS, b % SLOTS

        def taken(u):
            who, n = takes[u]
            return (s_taken_by_act if who == "a" else s_taken_by_dve), n

        def head_squares(n):
            return (xc, sq)[n % 8 // 4][0:QKD, 2 * (n % 4):2 * (n % 4) + 2]

        def first_weights(n):
            place = (big[:, 0:8], big[:, 8:16], big[:, 16:24], proj[:, 0:8], proj[:, 8:16], proj[:, 16:24],
                     h[:], rec[:, 0:8])[n]
            return place.rearrange("p a b -> p (a b)")

        block = ctx.enter_context(nc.Block())

        @block.sync
        def _(sp):
            sp.dma_start(cols[:], I["cols"]).then_inc(s_cols_dma, 16)
            sp.dma_start(x[:], I["x"]).then_inc(s_x_dma, 16)
            sp.dma_start(rec[:, 8:16], I["ctx"]).then_inc(s_ctx_dma, 16)
            for dst, src in ((vec[:], I["vec"]), (ada_b[:], I["ada_b"]), (ident[:], I["ident"]), (bias[0:QKD, 0], I["rope"]), (bias[0:QKD, 1, 0, 0:QKD], I["rot"]),
                             (sil[0:BUCKETS], I["onehot"]), (work[0:BUCKETS], I["relb"])):
                sp.dma_start(dst, src).then_inc(s_tables_dma, 16)
            for n in range(FIRST_N):
                sp.dma_start(first_weights(n), I["ada_first"][n]).then_inc(s_ada_first_dma[n], 16)

            def load(ph, i, j):
                n, slot = ph.first + j, (ph.first + j) % SLOTS
                if not isinstance(i, int):
                    sp.wait_ge(s_unit, i * SLOTS * ph.per + (ph.unit0 + (j + 1 - SLOTS) * ph.per))
                elif i * SLOTS + n >= SLOTS:
                    sp.wait_ge(s_unit, unit_end[i * SLOTS + n - SLOTS])
                sp.dma_start(ring[slot][:, 0:ph.cols], ph.src[i * SLOTS + j]).then_inc(s_weights[slot], 16)

            for ph in phases:
                whole = ph.nb // SLOTS if ph.nb >= 3 * SLOTS else 1
                for j in range(min(SLOTS, ph.nb)):
                    load(ph, 0, j)
                if whole > 1:
                    with sp.Fori(1, whole) as i:
                        for j in range(SLOTS):
                            load(ph, i, j)
                for b in range(whole * SLOTS, ph.nb):
                    load(ph, b // SLOTS, b % SLOTS)
                if ph.name == (0, "in_b"):
                    for dst, src in ((masks[:], I["masks"]), (causal[:], I["causal"]), (poolw[:], I["poolw"])):
                        sp.dma_start(dst, src).then_inc(s_mixer_tables_dma, 16)
                if ph.name == (0, "wo"):
                    sp.wait_ge(s_rope_tables_used, nth(sp, s_rope_tables_used))
                    sp.wait_ge(s_bias_rows_dma, nth(sp, s_bias_rows_dma, AH))
                    for a in range(AH):
                        for tt in range(TT):
                            at = 255 - P * tt
                            src = bias_rows[a, at:at + P * 511].rearrange("(p s) -> p s", s=511)[:, 0:T]
                            sp.dma_start(bias[:, a, tt, :], src).then_inc(s_bias_dma, 16)
            if len(subs) > FIRST2:
                sp.wait_ge(s_x_new, nth(sp, s_x_new, KD * (len(subs) - FIRST2)))
            sp.wait_ge(*taken(len(takes) - 1))
            sp.dma_start(out, x[:]).then_inc(s_result_dma, 16)
            sp.wait_ge(s_result_dma, nth(sp, s_result_dma))

        @block.gpsimd
        def _(pool):
            def load(n):
                if n < ADA_N * len(subs) - FIRST_GATE:
                    pool.dma_start(ada_ring[n % 2][:], I["ada"][n]).then_inc(s_ada_dma[n % 2], 16)

            load(0)
            load(1)
            pool.memset(ones[:], 1.0).then_inc(s_fills, 1)
            pool.memset(eps[:, 0:1], 1e-6).then_inc(s_fills, 1)
            pool.memset(eps[:, 1:2], 1e-5).then_inc(s_fills, 1)
            pool.wait_ge(s_silu_c, nth(pool, s_silu_c))

            def product(w, c, dst):
                cb = csil[:, c, :].unsqueeze(2).broadcast_to([P, KD, ADA_C])
                pool.tensor_tensor(w, w, cb, ALU.mult).then_inc(s_pool_chain, 1)
                pool.wait_ge(s_pool_chain, nth(pool, s_pool_chain))
                pool.tensor_tensor(w[:, 0:4], w[:, 0:4], w[:, 4:8], ALU.add).then_inc(s_pool_chain, 1)
                pool.wait_ge(s_pool_chain, nth(pool, s_pool_chain))
                pool.tensor_tensor(w[:, 0:2], w[:, 0:2], w[:, 2:4], ALU.add).then_inc(s_pool_chain, 1)
                pool.wait_ge(s_pool_chain, nth(pool, s_pool_chain))
                pool.tensor_tensor(dst, w[:, 0], w[:, 1], ALU.add).then_inc(s_pool_chain, 1)
                pool.wait_ge(s_pool_chain, nth(pool, s_pool_chain))

            for s in range(len(subs)):
                if s > 1:
                    pool.wait_ge(s_modulation_summed, nth(pool, s_modulation_summed))
                for b in range(0 if s else FIRST_GATE, ADA_N):
                    n = s * ADA_N + b - FIRST_GATE
                    if s == 1 and b == 0:
                        pool.wait_ge(s_first_summed, 1)
                    if s == 1 and b == FIRST_GATE:
                        pool.wait_ge(s_first_summed, 2)
                    pool.wait_ge(s_ada_dma[n % 2], (n // 2 + 1) * 16)
                    product(ada_ring[n % 2][:], 0 if s < FIRST2 else 2, ada_sum[:, b * ADA_C:(b + 1) * ADA_C])
                    load(n + 2)
                pool.sem_inc(s_ada_ready, 1)

        @block.scalar
        def _(act):
            A = nc.scalar.activation

            def take(u, pairs):
                act.wait_ge(s_unit, (u) + 1)
                for dst, lo, hi, p0, p1 in pairs:
                    src = lin[u % NBANK][p0:p1, lo:hi]
                    if len(dst.shape) == 3:
                        src = src.rearrange("p (a b) -> p a b", a=dst.shape[1])
                    ins = A(dst, src, ACT.Copy)
                ins.then_inc(s_taken_by_act, 1)

            act.wait_ge(s_cols_dma, nth(act, s_cols_dma))
            A(csil[:], cols[:], ACT.Silu).then_inc(s_silu_c, 1)
            act.wait_ge(s_fills, nth(act, s_fills, 3))
            act.wait_ge(s_bound_logits, nth(act, s_bound_logits))
            A(lbv[:, 1:3], lbv[:, 1:3], ACT.Exp).then_inc(s_bound_exps, 1)

            def bias_rows_out():
                for a in range(AH):
                    act.wait_ge(s_bias_row_summed, nth(act, s_bias_row_summed))
                    rows = tok[:].rearrange("p a b -> p (a b)")[:, a * 512:(a + 1) * 512]
                    A(rows, pa[a][:], ACT.Copy).then_inc(s_bias_row_taken, 1)
                    act.wait_ge(s_bias_row_taken, nth(act, s_bias_row_taken))
                    act.dma_start(bias_rows[a, 0:P * 512].rearrange("(p s) -> p s", s=512), rows)\
                       .then_inc(s_bias_rows_dma, 16)

            def deviation(e=0):
                act.wait_ge(s_sums_over_features, nth(act, s_sums_over_features))
                A(sd[:], pstat[:, 0:T], ACT.Sqrt, scale=1.0 / D, bias=eps[:, e:e + 1]).then_inc(s_deviation, 1)

            def squares(dst, src, last_unit=None):
                for k in range(0, KD, 2):
                    if last_unit is not None:
                        act.wait_ge(*taken(last_unit - (KD - 1) + k + 1))
                    A(dst[:, k:k + 2], src[:, k:k + 2], ACT.Square).then_inc(s_squares, 1)

            def col(name, n=0):
                return vec[:, VC[name] + n:VC[name] + n + 1]

            def mix(s):
                l = subs[:s].count("mix")
                u = unit0[s, "mproj"]
                for n in range(10):
                    take(u + n, [(proj[:, 2 * n:2 * n + 2], 0, 512, 0, P)])
                take(u + 10, [(proj[:, 20], 0, T, 0, P), (small[:, 0:TT * IH], T, T + TT * IH, 0, P)])
                for n in range(4):
                    take(u + 11 + n, [(tok[:, n % 2, (n // 2) * 512:(n // 2) * 512 + 512], 0, 512, 0, P)])
                take(u + 15, [(work[:], 0, 512, 0, P)])
                A(rec[:, 0:4], proj[:, HF:HF + 4], ACT.Sigmoid, scale=-1.0).then_inc(s_sigmoid_z, 1)
                A(proj[:, HQ:HQ + 4], proj[:, HQ:HQ + 4], ACT.Silu).then_inc(s_act_chain, 1)
                act.wait_ge(s_act_chain, nth(act, s_act_chain))
                A(proj[:, HG:HG + 4], proj[:, HG:HG + 4], ACT.Silu).then_inc(s_silu_q_and_out_gate, 1)
                act.wait_ge(s_silu_q_and_out_gate, nth(act, s_silu_q_and_out_gate))
                act.wait_ge(s_key_capped, nth(act, s_key_capped))
                A(proj[:, HF:HF + 4], proj[:, HF:HF + 4], ACT.Ln, scale=-1.0, bias=1.0).then_inc(s_log_forget, 1)
                for n in range(TT * IH // 2):
                    act.wait_ge(s_index_products, nth(act, s_index_products))
                    if n >= 2:
                        act.wait_ge(s_index_relu_used, nth(act, s_index_relu_used))
                    A(att[:, 2 * (n % 2):2 * (n % 2) + 2],
                      pa[n % 4][:].rearrange("p (a b) -> p a b", a=2), ACT.Relu).then_inc(s_index_relu, 1)
                act.wait_ge(s_unit, (u + 16) + 1)
                for i in range(2):
                    ps = col("pool_scale", 2 * l + i)
                    ins = A(yab[:, i], lin[(u + 16) % NBANK][:, i * T:i * T + T], ACT.Copy, scale=ps)
                ins.then_inc(s_taken_by_act, 1)
                g = [0]

                def gate_units(n):
                    for _ in range(n):
                        m = g[0]
                        g[0] += 1
                        act.wait_ge(s_unit, (u + 17 + m) + 1)
                        A(big[:, 2 * m:2 * m + 2],
                          lin[(u + 17 + m) % NBANK][:].rearrange("p (a b) -> p a b", a=2),
                          ACT.Sigmoid).then_inc(s_taken_by_act, 1)

                def exp_level(n):
                    act.wait_ge(s_exponents, nth(act, s_exponents))
                    A(xc[:, 4:8], xc[:, 0:4], ACT.Exp).then_inc(s_level_exps, 1)
                    if n == 6:
                        A(xc[:, 0:4], xc[:, 0:4], ACT.Exp, scale=-1.0).then_inc(s_level_exps, 1)

                gate_units(GATES_AT[0])
                act.wait_ge(s_index_relu_used, nth(act, s_index_relu_used, 2))
                exp_level(0)
                act.wait_ge(s_far_summed, nth(act, s_far_summed))
                A(sq[:, 4:6], pa[0][:].rearrange("p (a b) -> p a b", a=2), ACT.Copy).then_inc(s_far_scores, 1)
                for n in range(1, 7):
                    exp_level(n)
                    gate_units(GATES_AT[n])
                for tt in range(TT):
                    act.wait_ge(s_logits_max, nth(act, s_logits_max))
                    for a in range(AH):
                        ins = A(att[:, a], att[:, a], ACT.Exp, bias=small[:, 24 + a:25 + a],
                                accum_out=small[:, 28 + a:29 + a])
                    ins.then_inc(s_logits_exp, 1)
                    act.wait_ge(s_weights_turned, nth(act, s_weights_turned))
                    for kt in range(TT):
                        ins = A(att[:, 4 + 2 * kt:6 + 2 * kt], pa[2 * tt + kt][:].rearrange("p (a b) -> p a b", a=2),
                                ACT.Copy)
                    ins.then_inc(s_weights_turned_taken, 1)
                    act.wait_ge(s_attended, nth(act, s_attended))
                    ins = A(yab[:, 2:4, tt * P:tt * P + P], pstat[:, 0:T].rearrange("p (a b) -> p a b", a=2), ACT.Copy)
                    ins.then_inc(s_attended_taken, 1)
                    gate_units(GATES_AT[7 + tt])
                for tt in range(TT):
                    act.wait_ge(s_recurrence_out, nth(act, s_recurrence_out))
                    A(rec[:, 0:4, tt * P:tt * P + P], pa[tt][:].rearrange("p (a b) -> p a b", a=4), ACT.Copy).then_inc(s_act_chain, 1)
                    act.wait_ge(s_act_chain, nth(act, s_act_chain))
                A(rec[:, 4:8], rec[:, 0:4], ACT.Square).then_inc(s_recurrence_squares, 1)
                for n in range(2):
                    act.wait_ge(s_recurrence_sums, nth(act, s_recurrence_sums))
                    ins = A(rec[:, 8 + 2 * n:10 + 2 * n], pa[2 + n][:].rearrange("p (a b) -> p a b", a=2), ACT.Sqrt,
                            scale=1.0 / P, bias=eps[:, 0:1])
                ins.then_inc(s_recurrence_deviation, 1)
                gate_units(12 - g[0])

            for s, kind in enumerate(subs):
                before = unit0[s, FIRST_PHASE[kind]] - 1
                if s == 0:
                    act.wait_ge(s_x_dma, nth(act, s_x_dma))
                    act.wait_ge(s_ctx_dma, nth(act, s_ctx_dma))
                if s < FIRST2:
                    squares(sq, x, before if s else None)
                    deviation()
                if kind == "mla":
                    squares(sq, rec[:, 8:16])
                    act.wait_ge(s_rstd_made, nth(act, s_rstd_made))
                    deviation()
                    bias_rows_out()
                act.wait_ge(s_modulation_ready, nth(act, s_modulation_ready))
                for k in range(KD):
                    shift, scale = mod[:, k:k + 1], mod[:, 8 + k:9 + k]
                    if s < FIRST2:
                        act.wait_ge(s_x_scaled, nth(act, s_x_scaled))
                        A(h[:, k], xc[:, k], ACT.Identity, bias=shift).then_inc(s_h_ready, 1)
                    else:
                        if s == FIRST2:
                            act.wait_ge(*taken(before - (KD - 1) + k))
                        else:
                            act.wait_ge(s_x_new, nth(act, s_x_new))
                        A(h[:, k], x[:, k], ACT.Identity, scale=scale, bias=shift).then_inc(s_h_ready, 1)
                if kind == "mla":
                    for k in range(KD):
                        act.wait_ge(s_x_scaled, nth(act, s_x_scaled))
                        ins = A(rec[:, k], rec[:, 8 + k], ACT.Identity, bias=modc[:, k:k + 1])
                    ins.then_inc(s_context_ready, 1)
                    cq, ckv = proj[:, 12:15], proj[:, 15:19]
                    kpe = proj[64:96, 19:21]
                    u = unit0[s, "in_a"]
                    take(u, [(cq[:, 0:2], 0, 512, 0, P)])
                    take(u + 1, [(cq[:, 2], 0, T, 0, P)])
                    take(u + 2, [(ckv[:, 0:2], 0, 512, 0, P)])
                    take(u + 3, [(ckv[:, 2:4], 0, 512, 0, P)])
                    take(u + 4, [(kpe, 0, 512, 64, 96)])
                    A(sq[:, 0:3], cq, ACT.Square).then_inc(s_act_chain, 1)
                    act.wait_ge(s_act_chain, nth(act, s_act_chain))
                    A(sq[:, 3:7], ckv, ACT.Square).then_inc(s_latent_squares, 1)
                    for n in range(6):
                        take(u + 5 + n, [(proj[:, 2 * n:2 * n + 2], 0, 512, 0, P)])
                    act.wait_ge(s_latent_sums, nth(act, s_latent_sums))
                    A(sq[:, 0], pstat[:, 0:T], ACT.Sqrt, scale=1.0 / QL, bias=eps[:, 0:1])
                    A(sq[:, 1:3], pa[0][:].rearrange("p (a b) -> p a b", a=2), ACT.Sqrt,
                      scale=1.0 / KVL, bias=eps[:, 0:1]).then_inc(s_latent_deviation, 1)
                    qh = big[0:QKD, 16:24]
                    kh = big[:, 0:16].rearrange("p (h t) c -> p h (t c)", t=2)
                    u = unit0[s, "uq"]
                    act.wait_ge(s_latents_normed, nth(act, s_latents_normed))

                    def head_deviation(n):
                        act.wait_ge(s_head_sum, nth(act, s_head_sum))
                        A(head_squares(n), pa[n % 4][0:QKD].rearrange("p (a b) -> p a b", a=2), ACT.Sqrt,
                          scale=1.0 / QKD, bias=eps[0:QKD, 0:1]).then_inc(s_head_deviation, 1)

                    for n in range(12):
                        if n < 4:
                            take(u + n, [(qh[:, 2 * n:2 * n + 2], 0, 512, 0, QKD)])
                            v = qh[:, 2 * n:2 * n + 2]
                        else:
                            take(u + n, [(kh[0:NOPE, n - 4], 0, 512, 0, NOPE)])
                            v = big[0:QKD, 2 * n - 8:2 * n - 6]
                        if n == 4:
                            act.wait_ge(s_k_rope_part, nth(act, s_k_rope_part))
                        if n >= 8:
                            act.wait_ge(s_head_normed, n - 7)
                        act.wait_ge(*taken(u + n))
                        A(head_squares(n), v, ACT.Square).then_inc(s_head_squares, 1)
                        if n:
                            head_deviation(n - 1)
                    head_deviation(11)
                    act.wait_ge(s_bias_rows_dma, nth(act, s_bias_rows_dma, AH))
                    vt = tok[:].rearrange("p a (b c) -> p (a b) c", c=512)
                    for n in range(4):
                        take(u + 12 + n, [(vt[:, n], 0, 512, 0, P)])
                    for n in range(2 * MLA_H + 1):
                        if n < 2 * MLA_H:
                            act.wait_ge(s_row_max, nth(act, s_row_max))
                            p = sq[:, 2 * (n % 2):2 * (n % 2) + 2].rearrange("p a b -> p (a b)")
                            A(p, pa[n % 2][:], ACT.Exp, scale=QK_SCALE,
                              bias=small[:, 16 + n % 2:17 + n % 2],
                              accum_out=small[:, 18 + n % 2:19 + n % 2]).then_inc(s_row_exp, 1)
                        if n:
                            m = n - 1
                            act.wait_ge(s_p_turned, nth(act, s_p_turned))
                            A(sq[:, 4 + 2 * (m % 2):6 + 2 * (m % 2)],
                              pa[2][:].rearrange("p (a b) -> p a b", a=2), ACT.Copy).then_inc(s_p_turned_taken, 1)
                        if n > 1 and (n - 2) % 4 == 3:
                            pair = (n - 2) // 4
                            act.wait_ge(s_head_pair, nth(act, s_head_pair))
                            A(h[:, pair], (pa[3], pstat)[pair % 2][:, 0:T], ACT.Copy).then_inc(s_head_pair_taken, 1)
                    act.wait_ge(s_head_pair, nth(act, s_head_pair))
                    A(h[:, 3], pstat[:, 0:T], ACT.Copy).then_inc(s_head_pair_taken, 1)
                if kind == "ffn":
                    u0 = unit0[s, "w13"]
                    for i, j in blocks(act, by_name[s, "w13"]):
                        for c in range(2):
                            n = 2 * j + c
                            act.wait_ge(s_unit, (i * 2 * SLOTS + (u0 + n)) + 1)
                            act.wait_ge(s_taken_by_dve, i * 2 * SLOTS + (takes[u0 + n][1] - 2))
                            A(sil[:, n % 2], lin[(u0 + n) % NBANK][:, 0:T], ACT.Silu).then_inc(s_silu, 1)
                if kind == "fourier":
                    u = unit0[s, "dft"]
                    for n in range(8):
                        take(u + n, [(big[:, 2 * n:2 * n + 2], 0, 512, 0, P)])
                    for n in range(4):
                        take(u + 8 + n, [(h[:, 2 * n:2 * n + 2], 0, 512, 0, P)])
                if kind == "mix":
                    mix(s)
                if s >= FIRST2:
                    for k in range(0, KD, 2):
                        act.wait_ge(s_x_centred, nth(act, s_x_centred))
                        A(sq[:, k:k + 2], xc[:, k:k + 2], ACT.Square).then_inc(s_squares, 1)
                    deviation(1)
        @block.vector
        def _(dve):
            V = nc.vector

            def col(name, n=0):
                return vec[:, VC[name] + n:VC[name] + n + 1]

            def keep_modulation(s, sums):
                dve.wait_ge(s_modulation_summed, nth(dve, s_modulation_summed))
                V.tensor_tensor(ada_b[:, s], sums, ada_b[:, s], ALU.add).then_inc(s_modulation_kept, 1)
                dve.wait_ge(s_modulation_kept, nth(dve, s_modulation_kept))

            def first_products():
                dve.wait_ge(s_silu_c, nth(dve, s_silu_c))
                for n in range(FIRST_N):
                    if n in BY_PE:
                        continue
                    dve.wait_ge(s_ada_first_dma[n], 16)
                    w = first_weights(n).rearrange("p (m k c) -> p m k c", m=2, k=KD)
                    for k in range(KD):
                        for c, total in enumerate((ada_sum[:], att[:].rearrange("p a b -> p (a b)"))):
                            total = total[:, 2 * n * P:2 * (n + 1) * P].rearrange("p (m c) -> p m c", m=2)
                            f = csil[:, c, k:k + 1]
                            if k:
                                dve.wait_ge(s_dve_chain, nth(dve, s_dve_chain))
                                ins = V.scalar_tensor_tensor(total, w[:, :, k], f, total, ALU.mult, ALU.add)
                            else:
                                ins = V.tensor_scalar(total, w[:, :, k], f, None, ALU.mult)
                            ins.then_inc(s_dve_chain, 1)
                    dve.wait_ge(s_dve_chain, nth(dve, s_dve_chain, 2))
                dve.sem_inc(s_first_products, 1)

            def modulation(s):
                if s:
                    V.tensor_copy(mod[:], ada_b[:, s]).then_inc(s_dve_chain, 1)
                else:
                    dve.wait_ge(s_first_summed, nth(dve, s_first_summed))
                    V.tensor_tensor(mod[:, 0:16], pa[3][:, 0:32:2], ada_b[:, 0, 0:16], ALU.add).then_inc(s_dve_chain, 1)
                dve.wait_ge(s_dve_chain, nth(dve, s_dve_chain))
                scale, gate = mod[:, 8:16], mod[:, 16:24]
                if s < FIRST2:
                    g = vec[:, VC["norm_g"] + 8 * s:VC["norm_g"] + 8 * s + 8]
                    if s == 0:
                        V.tensor_tensor(modc[:], pa[3][:, 1:32:2], ada_b[:, 0, 0:16], ALU.add).then_inc(s_dve_chain, 1)
                        dve.wait_ge(s_dve_chain, nth(dve, s_dve_chain))
                        V.scalar_tensor_tensor(modc[:, 8:16], modc[:, 8:16], 1.0, g, ALU.add, ALU.mult).then_inc(s_dve_chain, 1)
                        dve.wait_ge(s_dve_chain, nth(dve, s_dve_chain))
                    V.scalar_tensor_tensor(scale, scale, 1.0, g, ALU.add, ALU.mult).then_inc(s_modulation_ready, 1)
                    dve.wait_ge(s_modulation_ready, nth(dve, s_modulation_ready))
                else:
                    V.tensor_scalar(gate, gate, 1.0, 0.5 if subs[s] == "ffn" else 1.0, ALU.add, ALU.mult).then_inc(s_dve_chain, 1)
                    dve.wait_ge(s_dve_chain, nth(dve, s_dve_chain))
                    V.tensor_scalar(scale, scale, 1.0, None, ALU.add).then_inc(s_modulation_ready, 1)
                    dve.wait_ge(s_modulation_ready, nth(dve, s_modulation_ready))

            def make_rstd(dst):
                dve.wait_ge(s_deviation, nth(dve, s_deviation))
                V.reciprocal(dst, sd[:]).then_inc(s_rstd_made, 1)
                dve.wait_ge(s_rstd_made, nth(dve, s_rstd_made))

            def residual(s, name):
                if s + 1 < len(subs):
                    keep_modulation(s + 1, pa[3][:, 0:24])
                u0 = unit0[s, name]
                ph = by_name[s, name]
                per = KD // ph.nb
                for i, j in blocks(dve, ph):
                    for c in range(per):
                        n = j * per + c
                        dve.wait_ge(s_unit, (i * SLOTS * per + (u0 + n)) + 1)
                        m = i * SLOTS * per + n
                        gate = mod[:, 16 + m:17 + m] if isinstance(m, int) else mod[:, bass.ds(m + 16, 1)]
                        xt = x[:, m] if isinstance(m, int) else x[:, bass.ds(m, 1), :].rearrange("p a b -> p (a b)")
                        ins = V.scalar_tensor_tensor(xt, lin[(u0 + n) % NBANK][:, 0:T], gate, xt, ALU.mult, ALU.add)
                        ins.then_inc(s_taken_by_dve, 1)
                dve.wait_ge(*taken(u0 + KD - 1))

            def mla(s):
                dve.wait_ge(s_first_summed, nth(dve, s_first_summed))
                V.tensor_tensor(mod[:, 16:24], pa[3][:, 32:40], ada_b[:, 0, 16:24], ALU.add).then_inc(s_dve_chain, 1)
                dve.wait_ge(s_dve_chain, nth(dve, s_dve_chain))
                cq, ckv = proj[:, 12:15], proj[:, 15:19]
                dve.wait_ge(s_latent_deviation, nth(dve, s_latent_deviation))
                V.reciprocal(sq[:, 0:3], sq[:, 0:3]).then_inc(s_dve_chain, 1)
                dve.wait_ge(s_dve_chain, nth(dve, s_dve_chain))
                for k in range(KQ):
                    V.scalar_tensor_tensor(cq[:, k], cq[:, k], col("q_norm", k), sq[:, 0], ALU.mult, ALU.mult)
                for k in range(KKV):
                    kv = ckv[:, 2 * k:2 * k + 2]
                    ins = V.scalar_tensor_tensor(kv, kv, col("kv_norm", k), sq[:, 1:3], ALU.mult, ALU.mult)
                ins.then_inc(s_latents_normed, 1)
                u = unit0[s, "in_a"]
                dve.wait_ge(*taken(u + 4))
                kh = big[:, 0:16].rearrange("p (h t) c -> p h (t c)", t=2)
                kpe = proj[64:96, 19:21].rearrange("p a b -> p (a b)").unsqueeze(1).broadcast_to([ROPE, MLA_H, 2 * T])
                V.tensor_copy(kh[64:96], kpe).then_inc(s_k_rope_part, 1)
                dve.wait_ge(*taken(u + 10))
                zp = rec[:].rearrange("p a b -> p (a b)")[:, 0:KC * (T + 2)].rearrange("p (k t) -> p k t", k=KC)
                y = rec[:, 8:12]
                V.memset(zp[:, :, 0:1], 0.0).then_inc(s_dve_chain, 1)
                dve.wait_ge(s_dve_chain, nth(dve, s_dve_chain))
                V.memset(zp[:, :, T + 1:T + 2], 0.0).then_inc(s_dve_chain, 1)
                dve.wait_ge(s_dve_chain, nth(dve, s_dve_chain))
                V.tensor_tensor(zp[:, :, 1:T + 1], proj[:, 4:8], proj[:, 8:12], ALU.mult).then_inc(s_dve_chain, 1)
                dve.wait_ge(s_dve_chain, nth(dve, s_dve_chain))
                for k in range(KC):
                    ins = V.tensor_scalar(y[:, k], zp[:, k, 0:T], col("conv", k), None, ALU.mult)
                ins.then_inc(s_dve_chain, 1)
                dve.wait_ge(s_dve_chain, nth(dve, s_dve_chain))
                for w in (1, 2):
                    for k in range(KC):
                        ins = V.scalar_tensor_tensor(y[:, k], zp[:, k, w:w + T], col("conv", w * KC + k), y[:, k],
                                                     ALU.mult, ALU.add)
                    ins.then_inc(s_dve_chain, 1)
                    dve.wait_ge(s_dve_chain, nth(dve, s_dve_chain))
                V.tensor_tensor(h[:, 4:8], proj[:, 0:4], y, ALU.mult).then_inc(s_conv_done, 1)
                for n in range(12):
                    dve.wait_ge(s_head_deviation, nth(dve, s_head_deviation))
                    r = head_squares(n)
                    v = big[0:QKD, 16 + 2 * n:18 + 2 * n] if n < 4 else big[0:QKD, 2 * n - 8:2 * n - 6]
                    V.reciprocal(r, r).then_inc(s_dve_chain, 1)
                    dve.wait_ge(s_dve_chain, nth(dve, s_dve_chain))
                    gain = vec[0:QKD, VC["q_gain"] + (n >= 4):VC["q_gain"] + (n >= 4) + 1]
                    V.scalar_tensor_tensor(v, v, gain, r, ALU.mult, ALU.mult).then_inc(s_head_normed, 1)
                cos = bias[64:96, 0, 0].unsqueeze(1).broadcast_to([ROPE, 2, T])
                sin = bias[64:96, 0, 1].unsqueeze(1).broadcast_to([ROPE, 2, T])
                dve.wait_ge(s_head_normed, nth(dve, s_head_normed, 12))
                for n in range(8):
                    dve.wait_ge(s_half_turned, nth(dve, s_half_turned))
                    v = big[64:96, 16 + 2 * n:18 + 2 * n] if n < 4 else big[64:96, 4 * (n - 4):4 * (n - 4) + 3:2]
                    t = sq[64:96, 0:2]
                    ps = pa[n % 4][64:96].rearrange("p (a b) -> p a b", a=2)
                    V.tensor_tensor(t, ps, sin, ALU.mult)
                    V.tensor_tensor(v, v, cos, ALU.mult).then_inc(s_dve_chain, 1)
                    dve.wait_ge(s_dve_chain, nth(dve, s_dve_chain))
                    V.tensor_tensor(v, v, t, ALU.add).then_inc(s_rotated, 1)
                    dve.wait_ge(s_rotated, nth(dve, s_rotated))
                dve.sem_inc(s_rope_tables_used, 1)
                for n in range(2 * MLA_H + 1):
                    if n < 2 * MLA_H:
                        dve.wait_ge(s_logits, nth(dve, s_logits))
                        V.tensor_reduce(small[:, 20 + n % 2:21 + n % 2], pa[n % 2][:], AX, ALU.max, negate=True).then_inc(s_dve_chain, 1)
                        dve.wait_ge(s_dve_chain, nth(dve, s_dve_chain))
                        V.tensor_scalar(small[:, 16 + n % 2:17 + n % 2],
                                        small[:, 20 + n % 2:21 + n % 2], QK_SCALE, None, ALU.mult).then_inc(s_row_max, 1)
                    if n:
                        m = (n - 1) % 2
                        dve.wait_ge(s_row_exp, nth(dve, s_row_exp))
                        V.reciprocal(small[:, 22 + m:23 + m], small[:, 18 + m:19 + m]).then_inc(s_dve_chain, 1)
                        dve.wait_ge(s_dve_chain, nth(dve, s_dve_chain))
                        p = sq[:, 2 * m:2 * m + 2]
                        V.tensor_scalar(p, p, small[:, 22 + m:23 + m], None, ALU.mult).then_inc(s_p_normed, 1)

            def mix(s):
                l = subs[:s].count("mix")
                key, run, q_l, k_l = rec[:, 0:4], rec[:, 4:8], rec[:, 8:12], rec[:, 12:16]
                dve.wait_ge(s_mixer_tables_dma, 3 * 16)
                dve.wait_ge(s_sigmoid_z, nth(dve, s_sigmoid_z))
                for a in range(HH):
                    ins = V.tensor_scalar(key[:, a], key[:, a], lbv[:, 6 + l, a:a + 1], None, ALU.mult)
                ins.then_inc(s_dve_chain, 1)
                dve.wait_ge(s_dve_chain, nth(dve, s_dve_chain))
                V.tensor_scalar(proj[:, HF:HF + 4], key, KEY_MAX, None, ALU.min).then_inc(s_key_capped, 1)
                V.memset(rec[:, 8:16], 0.0).then_inc(s_dve_chain, 1)
                dve.wait_ge(s_dve_chain, nth(dve, s_dve_chain))
                dve.wait_ge(s_log_forget, nth(dve, s_log_forget))
                for a in range(HH):
                    ins = V.tensor_tensor_scan(run[:, a], ones[:, 0:1].broadcast_to([P, T]), proj[:, HF + a], 0.0,
                                               ALU.mult, ALU.add)
                ins.then_inc(s_dve_chain, 1)
                dve.wait_ge(s_dve_chain, nth(dve, s_dve_chain))
                for n in range(TT * IH // 2):
                    dve.wait_ge(s_index_relu, nth(dve, s_index_relu))
                    tt, acc = n // 4, sil[:, n // 4]
                    for c in range(2):
                        r = att[:, 2 * (n % 2) + c]
                        head = tt * IH + 4 * (n % 4 // 2) + 2 * c + n % 2
                        w = small[:, head:head + 1]
                        if n % 4 == 0 and c == 0:
                            V.tensor_scalar(acc, r, w, None, ALU.mult).then_inc(s_dve_chain, 1)
                            dve.wait_ge(s_dve_chain, nth(dve, s_dve_chain))
                        elif c == 0:
                            V.scalar_tensor_tensor(acc, r, w, acc, ALU.mult, ALU.add).then_inc(s_dve_chain, 1)
                            dve.wait_ge(s_dve_chain, nth(dve, s_dve_chain))
                        else:
                            V.scalar_tensor_tensor(acc, r, w, acc, ALU.mult, ALU.add).then_inc(s_index_relu_used, 1)
                            dve.wait_ge(s_index_relu_used, nth(dve, s_index_relu_used))
                dve.wait_ge(s_unit, (unit0[s, "pool"] + 1) + 1)
                V.tensor_scalar(work[:], causal[:], -1.0, -UNSEEN, ALU.add, ALU.mult).then_inc(s_dve_chain, 1)
                dve.wait_ge(s_dve_chain, nth(dve, s_dve_chain))
                V.scalar_tensor_tensor(sil[:], sil[:], IDX_SCALE, causal[:], ALU.mult, ALU.mult).then_inc(s_dve_chain, 1)
                dve.wait_ge(s_dve_chain, nth(dve, s_dve_chain))
                V.tensor_tensor(sil[:], sil[:], work[:], ALU.add).then_inc(s_dve_chain, 1)
                dve.wait_ge(s_dve_chain, nth(dve, s_dve_chain))
                for r in range(TOPK // 8):
                    for tt in range(TT):
                        src = sil[:, tt] if r == 0 else work[:, tt]
                        V.max(top8[:, 8 * tt:8 * tt + 8], src).then_inc(s_dve_chain, 1)
                        dve.wait_ge(s_dve_chain, nth(dve, s_dve_chain))
                        V.match_replace(work[:, tt], top8[:, 8 * tt:8 * tt + 8], src, TAKEN).then_inc(s_dve_chain, 1)
                        dve.wait_ge(s_dve_chain, nth(dve, s_dve_chain))
                V.scalar_tensor_tensor(sil[:], work[:], TAKEN, causal[:], ALU.is_equal, ALU.mult).then_inc(s_dve_chain, 1)
                dve.wait_ge(s_dve_chain, nth(dve, s_dve_chain))
                V.tensor_scalar(sil[:], sil[:], -1.0, 1e30, ALU.add, ALU.mult).then_inc(s_dve_chain, 1)
                dve.wait_ge(s_dve_chain, nth(dve, s_dve_chain))

                dve.wait_ge(s_silu_q_and_out_gate, nth(dve, s_silu_q_and_out_gate))
                q = proj[:, HQ:HQ + 4]

                def halves(v, m):
                    return v.rearrange("p a b -> p (a b)").rearrange("p (b r) -> p b r", r=2 * m)

                def exponents(n):
                    d = xc[:, 0:4]
                    if n < 6:
                        m = ([P] + LEVELS)[n]
                        a, e = halves(run, m), halves(d, m)
                        mid = a[:, :, m - 1:m].broadcast_to([P, a.shape[1], m])
                        V.tensor_tensor(e[:, :, 0:m], mid, a[:, :, 0:m], ALU.subtract)
                        V.tensor_tensor(e[:, :, m:2 * m], a[:, :, m:2 * m], mid, ALU.subtract).then_inc(s_exponents, 1)
                    else:
                        a, e = halves(run, 2), halves(d, 2)
                        mid = a[:, :, 1:2].broadcast_to([P, a.shape[1], 4])
                        V.tensor_tensor(e, a, mid, ALU.subtract).then_inc(s_exponents, 1)

                def add_level(n):
                    for tt in range(TT):
                        dve.wait_ge(s_level_scores, nth(dve, s_level_scores))
                        ps = pa[2 * (n % 2) + tt][:].rearrange("p (a b) -> p a b", a=HH)
                        mask = masks[:, n - 1].unsqueeze(1).broadcast_to([P, HH, P])
                        acc, t = sq[:, 2 * tt:2 * tt + 2], sq[:, 6:8]
                        four = lambda v: v.rearrange("p a b -> p (a b)").rearrange("p (a b) -> p a b", a=HH)
                        if n == 1:
                            V.tensor_tensor(four(acc), ps, mask, ALU.mult).then_inc(s_level_added, 1)
                            dve.wait_ge(s_level_added, nth(dve, s_level_added))
                        else:
                            V.tensor_tensor(four(t), ps, mask, ALU.mult).then_inc(s_dve_chain, 1)
                            dve.wait_ge(s_dve_chain, nth(dve, s_dve_chain))
                            V.tensor_tensor(acc, acc, t, ALU.add).then_inc(s_level_added, 1)
                            dve.wait_ge(s_level_added, nth(dve, s_level_added))

                exponents(0)
                for n in range(7):
                    dve.wait_ge(s_level_exps, nth(dve, s_level_exps, 2 if n == 6 else 1))
                    if n:
                        dve.wait_ge(s_level_products, nth(dve, s_level_products))
                    if n < 6:
                        m = ([P] + LEVELS)[n]
                        e = halves(xc[:, 4:8], m)
                        V.tensor_tensor(halves(q_l, m)[:, :, m:2 * m], halves(q, m)[:, :, m:2 * m], e[:, :, m:2 * m],
                                        ALU.mult)
                        V.tensor_tensor(halves(k_l, m)[:, :, 0:m], halves(key, m)[:, :, 0:m],
                                        e[:, :, 0:m], ALU.mult).then_inc(s_level_ready, 1)
                        exponents(n + 1)
                    else:
                        V.tensor_tensor(q_l, q, xc[:, 4:8], ALU.mult)
                        V.tensor_tensor(k_l, key, xc[:, 0:4], ALU.mult).then_inc(s_level_ready, 1)
                    if n > 1:
                        add_level(n - 1)
                dve.wait_ge(s_level_products, nth(dve, s_level_products))
                add_level(6)

                if l == 0:
                    dve.wait_ge(s_bias_dma, nth(dve, s_bias_dma, AH * TT))
                for tt in range(TT):
                    lg = att[:, 0:4]
                    if tt:
                        dve.wait_ge(s_weights_turned_taken, nth(dve, s_weights_turned_taken))
                    for pair in range(2):
                        dve.wait_ge(s_attention_logits, nth(dve, s_attention_logits))
                        ps = pa[2 * tt + pair][:].rearrange("p (a b) -> p a b", a=2)
                        ins = V.scalar_tensor_tensor(lg[:, 2 * pair:2 * pair + 2], ps, AT_SCALE,
                                                     bias[:, pair:pair + 3:2, tt], ALU.mult, ALU.add)
                    ins.then_inc(s_dve_chain, 1)
                    dve.wait_ge(s_dve_chain, nth(dve, s_dve_chain))
                    V.tensor_tensor(lg, lg, sil[:, tt].unsqueeze(1).broadcast_to([P, AH, T]), ALU.add).then_inc(s_dve_chain, 1)
                    dve.wait_ge(s_dve_chain, nth(dve, s_dve_chain))
                    V.tensor_reduce(small[:, 24:28], lg, AX, ALU.max, negate=True).then_inc(s_logits_max, 1)
                    dve.wait_ge(s_logits_exp, nth(dve, s_logits_exp))
                    V.reciprocal(small[:, 32:36], small[:, 28:32]).then_inc(s_dve_chain, 1)
                    dve.wait_ge(s_dve_chain, nth(dve, s_dve_chain))
                    V.tensor_tensor(
 lg, lg, small[:, 32:36].unsqueeze(2).broadcast_to([P, AH, T]), ALU.mult).then_inc(s_weights_ready, 1)

                dve.wait_ge(s_recurrence_deviation, nth(dve, s_recurrence_deviation))
                o, r = rec[:, 0:4], rec[:, 8:12]
                V.reciprocal(r, r).then_inc(s_dve_chain, 1)
                dve.wait_ge(s_dve_chain, nth(dve, s_dve_chain))
                V.tensor_tensor(o, o, r, ALU.mult).then_inc(s_dve_chain, 1)
                dve.wait_ge(s_dve_chain, nth(dve, s_dve_chain))
                for a in range(HH):
                    ins = V.scalar_tensor_tensor(o[:, a], o[:, a], col("hgrn_norm", l * HH + a), proj[:, HG + a],
                                                 ALU.mult, ALU.mult)
                ins.then_inc(s_recurrence_ready, 1)
                dve.wait_ge(s_attended_taken, nth(dve, s_attended_taken, 2))
                dve.wait_ge(s_weights_turned_taken, nth(dve, s_weights_turned_taken))

                u = unit0[s, "branch"]
                for m in range(KD):
                    dve.wait_ge(s_unit, (u + 2 * m) + 1)
                    if m == 0:
                        dve.wait_ge(*taken(u - 1))
                    t = att[:, 0:2]
                    gates = big[:, m:m + KD + 1:KD]
                    V.tensor_tensor(t, lin[(u + 2 * m) % NBANK][:].rearrange("p (a b) -> p a b", a=2),
                                    gates, ALU.mult).then_inc(s_taken_by_dve, 1)
                    dve.wait_ge(s_unit, (u + 2 * m + 1) + 1)
                    V.tensor_tensor(att[:, 2], lin[(u + 2 * m + 1) % NBANK][:, 0:T],
                                    big[:, 2 * KD + m], ALU.mult).then_inc(s_taken_by_dve, 1)
                    dve.wait_ge(*taken(u + 2 * m + 1))
                    V.tensor_tensor(att[:, 0], att[:, 0], att[:, 1], ALU.add).then_inc(s_dve_chain, 1)
                    dve.wait_ge(s_dve_chain, nth(dve, s_dve_chain))
                    ins = V.tensor_tensor(h[:, m], att[:, 0], att[:, 2], ALU.add)
                    ins.then_inc(s_branches_merged, 1)
                    dve.wait_ge(s_branches_merged, nth(dve, s_branches_merged))

            dve.wait_ge(s_tables_dma, nth(dve, s_tables_dma, 7))
            dve.wait_ge(s_x_dma, nth(dve, s_x_dma))
            lb = [vec[:, VC["lb"] + HH * l:VC["lb"] + HH * l + HH] for l in range(DEPTH)]
            V.tensor_tensor(lbv[:, 0], lb[0], lb[1], ALU.max).then_inc(s_dve_chain, 1)
            dve.wait_ge(s_dve_chain, nth(dve, s_dve_chain))
            V.tensor_tensor(lbv[:, 1], lb[0], lbv[:, 0], ALU.subtract).then_inc(s_dve_chain, 1)
            dve.wait_ge(s_dve_chain, nth(dve, s_dve_chain))
            V.tensor_tensor(lbv[:, 2], lb[1], lbv[:, 0], ALU.subtract).then_inc(s_dve_chain, 1)
            dve.wait_ge(s_dve_chain, nth(dve, s_dve_chain))
            V.tensor_copy(lbv[:, 3], lbv[:, 0]).then_inc(s_bound_logits, 1)
            dve.wait_ge(s_bound_exps, nth(dve, s_bound_exps))
            V.tensor_tensor(lbv[:, 3], lbv[:, 1], lbv[:, 2], ALU.add).then_inc(s_dve_chain, 1)
            dve.wait_ge(s_dve_chain, nth(dve, s_dve_chain))
            V.reciprocal(lbv[:, 4], lbv[:, 3]).then_inc(s_dve_chain, 1)
            dve.wait_ge(s_dve_chain, nth(dve, s_dve_chain))
            V.tensor_tensor(lbv[:, 1:3], lbv[:, 1:3], lbv[:, 4:5].broadcast_to([P, 2, HH]), ALU.mult).then_inc(s_dve_chain, 1)
            dve.wait_ge(s_dve_chain, nth(dve, s_dve_chain))
            V.tensor_tensor(lbv[:, 5], lbv[:, 1], lbv[:, 2], ALU.add).then_inc(s_dve_chain, 1)
            dve.wait_ge(s_dve_chain, nth(dve, s_dve_chain))
            V.tensor_tensor(lbv[:, 6], lbv[:, 1], lbv[:, 1], ALU.subtract).then_inc(s_dve_chain, 1)
            dve.wait_ge(s_dve_chain, nth(dve, s_dve_chain))
            V.tensor_tensor(lbv[:, 7], lbv[:, 5], lbv[:, 1], ALU.subtract).then_inc(s_dve_chain, 1)
            dve.wait_ge(s_dve_chain, nth(dve, s_dve_chain))
            V.tensor_scalar(lbv[:, 6:8], lbv[:, 6:8], -1.0, 1.0, ALU.mult, ALU.add).then_inc(s_dve_chain, 1)
            dve.wait_ge(s_dve_chain, nth(dve, s_dve_chain))

            for s, kind in enumerate(subs):
                if s == 0:
                    make_rstd(rstd[:])
                    make_rstd(yab[:, 0])
                    first_products()
                    modulation(0)
                elif s < FIRST2:
                    make_rstd(rstd[:])
                if s < FIRST2:
                    for k in range(KD):
                        V.scalar_tensor_tensor(xc[:, k], x[:, k], mod[:, 8 + k:9 + k], rstd[:], ALU.mult, ALU.mult)\
                         .then_inc(s_x_scaled, 1)
                else:
                    dve.wait_ge(s_h_ready, KD * (s + 1))
                    V.tensor_scalar(x[:], x[:], ALPHA, None, ALU.mult).then_inc(s_dve_chain, 1)
                    dve.wait_ge(s_dve_chain, nth(dve, s_dve_chain))
                if kind == "mla":
                    for k in range(KD):
                        V.scalar_tensor_tensor(rec[:, 8 + k], rec[:, 8 + k], modc[:, 8 + k:9 + k], yab[:, 0],
                                               ALU.mult, ALU.mult).then_inc(s_x_scaled, 1)
                    mla(s)
                    residual(s, "wo")
                if kind == "fourier":
                    residual(s, "wf")
                if kind == "ffn":
                    ffn = subs[:s].count("ffn")
                    u0 = unit0[s, "w13"]
                    for i, j in blocks(dve, by_name[s, "w13"]):
                        for c in range(2):
                            n = 2 * j + c
                            m = i * 2 * SLOTS + n
                            dst = big[:, m] if isinstance(m, int) else \
                                big[:, bass.ds(m, 1), :].rearrange("p a b -> p (a b)")
                            dve.wait_ge(s_silu, i * 2 * SLOTS + (ffn * KF + n + 1))
                            V.tensor_tensor(dst, sil[:, n % 2], lin[(u0 + n) % NBANK][:, T:2 * T],
                                            ALU.mult).then_inc(s_taken_by_dve, 1)
                    residual(s, "w2")
                if kind == "mix":
                    mix(s)
                    residual(s, "wout")
                if s + 1 < len(subs):
                    modulation(s + 1)
                if s >= FIRST2:
                    n = s - FIRST2
                    dve.wait_ge(s_mean_sums, nth(dve, s_mean_sums))
                    for k in range(0, KD, 2):
                        ps = pa[2][:, 0:T].unsqueeze(1).broadcast_to([P, 2, T])
                        V.scalar_tensor_tensor(xc[:, k:k + 2], ps, -1.0 / D, x[:, k:k + 2],
                                               ALU.mult, ALU.add).then_inc(s_x_centred, 1)
                    dve.wait_ge(s_x_centred, nth(dve, s_x_centred, 4))
                    make_rstd(rstd[:])
                    g, b = VC["ln_g"] + 8 * n, VC["ln_b"] + 8 * n
                    for k in range(KD + 1):
                        if k < KD:
                            V.scalar_tensor_tensor(xc[:, k], xc[:, k], vec[:, g + k:g + k + 1], rstd[:],
                                                   ALU.mult, ALU.mult).then_inc(s_dve_chain, 1)
                        if k:
                            dve.wait_ge(s_dve_chain, nth(dve, s_dve_chain))
                            V.tensor_scalar(x[:, k - 1], xc[:, k - 1], vec[:, b + k - 1:b + k], None,
                                            ALU.add).then_inc(s_x_new, 1)
                    dve.wait_ge(s_x_new, nth(dve, s_x_new, KD))

        @block.tensor
        def _(pe):
            mm = nc.tensor.matmul

            def slot_of(ph, i, j):
                n = ph.first + j
                pe.wait_ge(s_weights[n % SLOTS], (i + (n // SLOTS + 1)) * 16)
                return ring[n % SLOTS]

            def bank(u, i=0, per=0):
                if isinstance(i, int):
                    u, i = u + i * per, 0
                    if u >= NBANK:
                        pe.wait_ge(*taken(u - NBANK))
                    return lin[u % NBANK]
                s, n = taken(u - NBANK)
                pe.wait_ge(s, i * per + n)
                return lin[u % NBANK]

            def tile_sum(dst, w, at, nk, rhs, m=P, step=None):
                for k in range(nk):
                    lo = at + k * (step or m)
                    ins = mm(dst, w[:, lo:lo + m], rhs(k), start=k == 0, stop=k == nk - 1)
                return ins

            def over_features(src, nk, dst):
                for k in range(nk):
                    ins = mm(dst, ones[:], src(k), start=k == 0, stop=k == nk - 1)
                return ins

            def squares_summed():
                for k in range(KD):
                    if k % 2 == 0:
                        pe.wait_ge(s_squares, nth(pe, s_squares))
                    ins = mm(pstat[:, 0:T], ones[:], sq[:, k], start=k == 0, stop=k == KD - 1)
                ins.then_inc(s_sums_over_features, 1)

            tiles_of_h = [0]

            def h_tile(k):
                while tiles_of_h[0] <= s * KD + k:
                    pe.wait_ge(s_h_ready, nth(pe, s_h_ready))
                    tiles_of_h[0] += 1
                return h[:, k]

            def modulation_sums(dst):
                pe.wait_ge(s_ada_ready, nth(pe, s_ada_ready))
                for m in range(24):
                    ins = mm(dst[:, m:m + 1], ada_sum[:, m * P:m * P + P], ones[:, 0:1], start=True, stop=True)
                ins.then_inc(s_modulation_summed, 1)

            def next_modulation(s):
                if s + 1 < len(subs):
                    modulation_sums(pa[3])

            def first_modulation():
                for n in BY_PE:
                    pe.wait_ge(s_ada_first_dma[n], 16)
                    for m in (2 * n, 2 * n + 1):
                        for k in range(KD):
                            at = (m % 2 * KD + k) * P
                            mm(pa[3][:, 2 * m:2 * m + 2], first_weights(n)[:, at:at + P], csil[:, 0:2, k],
                               start=k == 0, stop=k == KD - 1)
                pe.wait_ge(s_first_products, nth(pe, s_first_products))
                for n in range(FIRST_N):
                    if n in BY_PE:
                        continue
                    for m in (2 * n, 2 * n + 1):
                        for c, total in enumerate((ada_sum[:], att[:].rearrange("p a b -> p (a b)"))):
                            ins = mm(pa[3][:, 2 * m + c:2 * m + c + 1], total[:, m * P:(m + 1) * P], ones[:, 0:1],
                                     start=True, stop=True)
                ins.then_inc(s_first_summed, 1)

            def project(s, name, rhs):
                ph = by_name[s, name]
                nk = ph.cols // (ph.per * P)
                for i, j in blocks(pe, ph):
                    w = slot_of(ph, i, j)
                    for c in range(ph.per):
                        b = bank(ph.unit0 + j * ph.per + c, i, SLOTS * ph.per)
                        tile_sum(b[:, 0:T], w, c * nk * P, nk, rhs).then_inc(s_unit, 1)

            def pairs(ph, i, j, units, rhs):
                w = slot_of(ph, i, j)
                for c in range(units):
                    b = bank(ph.unit0 + j * ph.per + c, i, SLOTS * ph.per)
                    for g in range(2):
                        ins = tile_sum(b[:, g * T:(g + 1) * T], w, (2 * c + g) * KD * P, KD, rhs)
                    ins.then_inc(s_unit, 1)

            def turn(dst, src):
                return nc.tensor.transpose(dst, src, ident[:])

            def mla(s):
                hc = rec[:, 0:8]
                u = unit0[s, "in_a"]
                lat, con = h_tile, (lambda k: hc[:, k])
                w = slot_of(by_name[s, "in_a"], 0, 0)
                b = bank(u)
                tile_sum(b[:, 0:T], w, 0, KD, lat)
                tile_sum(b[:, T:2 * T], w, KD * P, KD, lat).then_inc(s_unit, 1)
                tile_sum(bank(u + 1)[:, 0:T], w, 2 * KD * P, KD, lat).then_inc(s_unit, 1)
                pe.wait_ge(s_context_ready, nth(pe, s_context_ready))
                b = bank(u + 2)
                tile_sum(b[:, 0:T], w, 3 * KD * P, KD, lat)
                tile_sum(b[:, T:2 * T], w, 3 * KD * P, KD, con).then_inc(s_unit, 1)
                w = slot_of(by_name[s, "in_b"], 0, 0)
                b = bank(u + 3)
                tile_sum(b[:, 0:T], w, 0, KD, lat)
                tile_sum(b[:, T:2 * T], w, 0, KD, con).then_inc(s_unit, 1)
                b = bank(u + 4)
                tile_sum(b[64:96, 0:T], w, KD * P, KD, lat, ROPE)
                tile_sum(b[64:96, T:2 * T], w, KD * P, KD, con, ROPE).then_inc(s_unit, 1)
                for j in range(3):
                    pairs(by_name[s, "in_c"], 0, j, 2, lat)
                pe.wait_ge(s_ada_ready, nth(pe, s_ada_ready))
                for m in range(KD):
                    ins = mm(pa[3][:, 32 + m:33 + m], ada_sum[:, (16 + m) * P:(17 + m) * P], ones[:, 0:1],
                             start=True, stop=True)
                ins.then_inc(s_first_summed, 1)
                pe.wait_ge(s_latent_squares, nth(pe, s_latent_squares))
                over_features(lambda k: sq[:, k], KQ, pstat[:, 0:T])
                kv_sq = sq[:, 3:7].rearrange("p (k t) c -> p k (t c)", t=2)
                over_features(lambda k: kv_sq[:, k], KKV, pa[0][:]).then_inc(s_latent_sums, 1)
                pe.wait_ge(s_latents_normed, nth(pe, s_latents_normed))
                cq, ckv = proj[:, 12:15], proj[:, 15:19].rearrange("p (k t) c -> p k (t c)", t=2)
                def head_sum(n):
                    pe.wait_ge(s_head_squares, nth(pe, s_head_squares))
                    if n >= 4:
                        pe.wait_ge(s_head_deviation, nth(pe, s_head_deviation))
                    mm(pa[n % 4][0:QKD], ones[0:QKD, 0:QKD], head_squares(n).rearrange("p a b -> p (a b)"),
                       start=True, stop=True).then_inc(s_head_sum, 1)

                w = slot_of(by_name[s, "uq"], 0, 0)
                for n in range(4):
                    b = bank(u + 11 + n)
                    for c in range(2):
                        ins = tile_sum(b[0:QKD, c * T:(c + 1) * T], w, (2 * n + c) * QKD, KQ, lambda k: cq[:, k], QKD,
                                       MLA_H * QKD)
                    ins.then_inc(s_unit, 1)
                    if n:
                        head_sum(n - 1)
                w = slot_of(by_name[s, "ukv"], 0, 0)
                for n in range(MLA_H):
                    b = bank(u + 15 + n)
                    tile_sum(b[0:NOPE], w, n * NOPE, KKV, lambda k: ckv[:, k], NOPE, MLA_H * NOPE).then_inc(s_unit, 1)
                    head_sum(n + 3)
                for n in range(4):
                    b = bank(u + 23 + n)
                    for k in range(KKV):
                        ins = mm(b[:], ckv[:, k, n * P:(n + 1) * P], w[:, 1024 + k * 512:1536 + k * 512],
                                 start=k == 0, stop=k == KKV - 1)
                    ins.then_inc(s_unit, 1)
                    if n == 0:
                        head_sum(11)
                qh = big[0:QKD, 16:24].rearrange("p (h t) c -> p h (t c)", t=2)
                kh = big[:, 0:16].rearrange("p (h t) c -> p h (t c)", t=2)
                pe.wait_ge(s_head_deviation, nth(pe, s_head_deviation, 4))
                rot = bias[0:QKD, 1, 0, 0:QKD]
                for n in range(8):
                    pe.wait_ge(s_head_normed, nth(pe, s_head_normed, 1 if n < 4 else 2))
                    if n >= 4:
                        pe.wait_ge(s_rotated, nth(pe, s_rotated))
                    src = qh[:, n] if n < 4 else big[0:QKD, 4 * (n - 4):4 * (n - 4) + 3:2]
                    dst = pa[n % 4][0:QKD] if n < 4 else pa[n % 4][0:QKD].rearrange("p (a b) -> p a b", a=2)
                    mm(dst, rot, src, start=True, stop=True).then_inc(s_half_turned, 1)
                pe.wait_ge(s_rotated, nth(pe, s_rotated, 4))

                def logits(n):
                    a, tt = n // 2, n % 2
                    q = big[0:QKD, 16 + a, tt * P:tt * P + P]
                    mm(pa[n % 2][:], q, kh[0:QKD, a], start=True, stop=True).then_inc(s_logits, 1)

                def attend(n):
                    a, tt = n // 2, n % 2
                    pe.wait_ge(s_p_turned_taken, nth(pe, s_p_turned_taken))
                    if n % 4 == 0 and n >= 8:
                        pe.wait_ge(s_head_pair_taken, nth(pe, s_head_pair_taken))
                    lo = (a % 2) * VD
                    dst = (pa[3], pstat)[n // 4 % 2][lo:lo + VD, tt * P:tt * P + P]
                    vt = tok[:].rearrange("p a (b c) -> p (a b) c", c=512)
                    pt = sq[:, 4 + 2 * (n % 2):6 + 2 * (n % 2)].rearrange("p a (b c) -> p (a b) c", b=2)
                    for k in range(4):
                        ins = mm(dst, vt[:, k, a * VD:(a + 1) * VD], pt[:, k], start=k == 0, stop=k == 3)
                    if n % 4 == 3:
                        ins.then_inc(s_head_pair, 1)

                logits(0)
                for n in range(2 * MLA_H):
                    if n + 1 < 2 * MLA_H:
                        logits(n + 1)
                    pe.wait_ge(s_p_normed, nth(pe, s_p_normed))
                    if n:
                        attend(n - 1)
                    p = sq[:, 2 * (n % 2):2 * (n % 2) + 2].rearrange("p a (b c) -> p (a b) c", b=2)
                    for k in range(4):
                        ins = turn(pa[2][:, k * P:(k + 1) * P], p[:, k])
                    ins.then_inc(s_p_turned, 1)
                attend(2 * MLA_H - 1)
                pe.wait_ge(s_head_pair_taken, nth(pe, s_head_pair_taken, 2))
                pe.wait_ge(s_conv_done, nth(pe, s_conv_done))

            def fourier(s):
                u, ph = unit0[s, "dft"], by_name[s, "dft"]
                w = slot_of(ph, 0, 0)
                dft_d = w[:, 0:1024].rearrange("p (k n) -> p k n", k=2)
                dft_t = w[:, 1024:2048].rearrange("p (k c n) -> p k c n", k=2, c=2)
                fa = big[:, 0:16].rearrange("p (u a) b -> p u (a b)", a=2)
                for g in range(4):
                    for tt in range(TT):
                        b = bank(u + 2 * g + tt)
                        for k in range(2):
                            ins = mm(b[:], h_tile(2 * g + k)[:, tt * P:tt * P + P], dft_d[:, k], start=k == 0, stop=k == 1)
                        ins.then_inc(s_unit, 1)
                pe.wait_ge(*taken(u + 7))
                for g in range(4):
                    b = bank(u + 8 + g)
                    for j in range(2):
                        for n, (tt, c) in enumerate(((0, 0), (0, 1), (1, 0), (1, 1))):
                            ins = mm(b[:, j * T:(j + 1) * T], fa[:, 2 * g + tt, c * T + j * P:c * T + j * P + P],
                                     dft_t[:, tt, c], start=n == 0, stop=n == 3)
                    ins.then_inc(s_unit, 1)
                pe.wait_ge(*taken(u + 11))

            def mix(s):
                l = subs[:s].count("mix")
                rhs = h_tile
                pe.wait_ge(s_mixer_tables_dma, 3 * 16)
                u = unit0[s, "mproj"]
                for n in range(5):
                    pairs(by_name[s, "mproj"], n // SLOTS, n % SLOTS, 2, rhs)
                w = slot_of(by_name[s, "mlast"], 0, 0)
                b = bank(u + 10)
                tile_sum(b[:, 0:T], w, 0, KD, rhs)
                for tt in range(TT):
                    for k in range(KD):
                        ins = mm(b[:, T + tt * IH:T + (tt + 1) * IH], h[:, k, tt * P:tt * P + P],
                                 w[:, 1024 + k * IH:1024 + (k + 1) * IH], start=k == 0, stop=k == KD - 1)
                ins.then_inc(s_unit, 1)
                for n in range(4):
                    if n % 2 == 0:
                        w = slot_of(by_name[s, "mtok"], 0, n // 2)
                    b = bank(u + 11 + n)
                    tt = n % 2
                    for k in range(KD):
                        ins = mm(b[:], h[:, k, tt * P:tt * P + P], w[:, k * 512:(k + 1) * 512],
                                 start=k == 0, stop=k == KD - 1)
                    ins.then_inc(s_unit, 1)
                w = slot_of(by_name[s, "pool"], 0, 0)
                b = bank(u + 15)
                pe.wait_ge(*taken(u + 12))
                for g in range(4):
                    lo = (g % 2) * 64
                    for k in range(TT):
                        ins = mm(b[lo:lo + 64, (g // 2) * T:(g // 2 + 1) * T], tok[:, k, g * 64:(g + 1) * 64],
                                 w[:, (g * TT + k) * T:(g * TT + k + 1) * T], start=k == 0, stop=k == TT - 1)
                ins.then_inc(s_unit, 1)
                pe.wait_ge(*taken(u + 10))
                for n in range(TT * IH // 2):
                    if n >= 4:
                        pe.wait_ge(s_index_relu, nth(pe, s_index_relu))
                    tt, pair, lo = n // 4, n % 4 // 2, (n % 2) * 64
                    for c in range(2):
                        ins = mm(pa[n % 4][:, c * T:(c + 1) * T],
                                 proj[lo:lo + 64, QI + 2 * pair + c, tt * P:tt * P + P],
                                 proj[lo:lo + 64, KI], start=True, stop=True)
                    ins.then_inc(s_index_products, 1)
                pe.wait_ge(s_index_relu, nth(pe, s_index_relu, 4))
                pe.wait_ge(*taken(u + 15))
                b = bank(u + 16)
                for g in range(4):
                    lo = (g % 2) * 64
                    ins = mm(b[lo:lo + 64, (g // 2) * T:(g // 2 + 1) * T], poolw[lo:lo + 64, l, g // 2],
                             work[lo:lo + 64, g // 2], start=True, stop=True)
                ins.then_inc(s_unit, 1)

                ph = by_name[s, "gates"]
                g = [0]

                def gate_units(n):
                    for _ in range(n):
                        m = g[0]
                        g[0] += 1
                        if m % 2 == 0:
                            gw[0] = slot_of(ph, m // 2 // SLOTS, m // 2 % SLOTS)
                        b = bank(ph.unit0 + m)
                        for c in range(2):
                            ins = tile_sum(b[:, c * T:(c + 1) * T], gw[0], (2 * (m % 2) + c) * KD * P, KD, rhs)
                        ins.then_inc(s_unit, 1)

                gw = [None]
                q_l, k_l = rec[:, 8:12], rec[:, 12:16]
                gate_units(GATES_AT[0])
                pe.wait_ge(s_level_ready, nth(pe, s_level_ready))
                for a in range(HH):
                    ins = mm(pa[0][:, a * P:(a + 1) * P], k_l[:, a, 0:P], q_l[:, a, P:2 * P], start=True, stop=True)
                ins.then_inc(s_level_products, 1)
                pe.wait_ge(s_level_products, nth(pe, s_level_products))
                pe.sem_inc(s_far_summed, 1)
                for n in range(1, 7):
                    pe.wait_ge(s_level_ready, nth(pe, s_level_ready))
                    if n == 2:
                        pe.wait_ge(s_far_scores, nth(pe, s_far_scores))
                    if n >= 3:
                        pe.wait_ge(s_level_added, nth(pe, s_level_added, 2))
                    for tt in range(TT):
                        for a in range(HH):
                            ins = mm(pa[2 * (n % 2) + tt][:, a * P:(a + 1) * P], k_l[:, a, tt * P:tt * P + P],
                                     q_l[:, a, tt * P:tt * P + P], start=True, stop=True)
                        if tt == 0:
                            ins.then_inc(s_level_scores, 1)
                    ins.then_inc(s_level_products, 1)
                    pe.wait_ge(s_level_products, nth(pe, s_level_products))
                    pe.sem_inc(s_level_scores, 1)
                    gate_units(GATES_AT[n])
                pe.wait_ge(s_level_added, nth(pe, s_level_added, 4))
                for tt in range(TT):
                    for half in range(2):
                        lo = half * 64
                        for c in range(2):
                            ins = mm(pa[2 * tt + half][:, c * T:(c + 1) * T],
                                     proj[lo:lo + 64, AQ + c, tt * P:tt * P + P], proj[lo:lo + 64, AK + c],
                                     start=True, stop=True)
                        ins.then_inc(s_attention_logits, 1)
                for tt in range(TT):
                    pe.wait_ge(s_weights_ready, nth(pe, s_weights_ready))
                    for kt in range(TT):
                        for a in range(AH):
                            ins = turn(pa[2 * tt + kt][:, a * P:(a + 1) * P], att[:, a, kt * P:kt * P + P])
                    ins.then_inc(s_weights_turned, 1)
                    pe.wait_ge(s_weights_turned_taken, nth(pe, s_weights_turned_taken))
                    if tt:
                        pe.wait_ge(s_attended_taken, nth(pe, s_attended_taken))
                    for place, a in enumerate(HEAD_ORDER):
                        lo = (a % 2) * 64
                        for kt in range(TT):
                            pt = att[:, 4 + 2 * kt + place // 2, (place % 2) * P:(place % 2) * P + P]
                            ins = mm(pstat[lo:lo + 64, (a // 2) * P:(a // 2 + 1) * P],
                                     tok[:, kt, 256 + a * 64:320 + a * 64], pt, start=kt == 0, stop=kt == TT - 1)
                    ins.then_inc(s_attended, 1)
                    gate_units(GATES_AT[7 + tt])
                for tt in range(TT):
                    for a in range(HH):
                        dst = pa[tt][:, a * P:(a + 1) * P]
                        near = sq[:, 2 * tt + a // 2, (a % 2) * P:(a % 2) * P + P]
                        ins = mm(dst, tok[:, tt, 512 + a * P:512 + (a + 1) * P], near, start=True, stop=tt == 0)
                        if tt:
                            far = sq[:, 4 + a // 2, (a % 2) * P:(a % 2) * P + P]
                            ins = mm(dst, tok[:, 0, 512 + a * P:512 + (a + 1) * P], far, start=False, stop=True)
                    ins.then_inc(s_recurrence_out, 1)
                pe.wait_ge(s_recurrence_squares, nth(pe, s_recurrence_squares))
                for n in range(2):
                    mm(pa[2 + n][:], ones[:], rec[:, 4 + 2 * n:6 + 2 * n].rearrange(
                        "p a b -> p (a b)"), start=True, stop=True).then_inc(s_recurrence_sums, 1)
                gate_units(12 - g[0])
                pe.wait_ge(s_recurrence_ready, nth(pe, s_recurrence_ready))
                pe.wait_ge(s_attended_taken, nth(pe, s_attended_taken))
                pe.wait_ge(*taken(u + 16))
                ph = by_name[s, "branch"]
                for m in range(KD):
                    if m % 4 == 0:
                        w = slot_of(ph, 0, m // 4)
                    at = (m % 4) * KD * P
                    b = bank(ph.unit0 + 2 * m)
                    tile_sum(b[:, 0:T], w, at, 2, lambda k: yab[:, k])
                    tile_sum(b[:, T:2 * T], w, at + 2 * P, 2, lambda k: yab[:, 2 + k]).then_inc(s_unit, 1)
                    b = bank(ph.unit0 + 2 * m + 1)
                    tile_sum(b[:, 0:T], w, at + 4 * P, 4, lambda k: rec[:, k]).then_inc(s_unit, 1)
                pe.wait_ge(s_branches_merged, nth(pe, s_branches_merged, KD))


            def bias_rows_made():
                pe.wait_ge(s_tables_dma, nth(pe, s_tables_dma, 7))
                for a in range(AH):
                    rb = work[0:BUCKETS].rearrange("p a b -> p (a b)")[:, a * P:(a + 1) * P]
                    mm(pa[a][:], rb, sil[0:BUCKETS].rearrange("p a b -> p (a b)"),
                       start=True, stop=True).then_inc(s_bias_row_summed, 1)
                pe.wait_ge(s_bias_row_taken, nth(pe, s_bias_row_taken, AH))

            pe.wait_ge(s_fills, nth(pe, s_fills, 3))
            for s, kind in enumerate(subs):
                if s < FIRST2:
                    squares_summed()
                if kind == "mla":
                    squares_summed()
                if s == 0:
                    bias_rows_made()
                    pe.wait_ge(s_silu_c, nth(pe, s_silu_c))
                    first_modulation()
                if kind == "mla":
                    mla(s)
                    next_modulation(s)
                    project(s, "wo", lambda k: h[:, k])
                if kind == "fourier":
                    fourier(s)
                    next_modulation(s)
                    project(s, "wf", lambda k: h[:, k])
                if kind == "ffn":
                    ph = by_name[s, "w13"]
                    for i, j in blocks(pe, ph):
                        if isinstance(i, int) and j == 0:
                            next_modulation(s)
                        pairs(ph, i, j, 2, h_tile)
                    pe.wait_ge(*taken(unit0[s, "w2"] - 1))
                    project(s, "w2", lambda k: big[:, k])
                if kind == "mix":
                    mix(s)
                    next_modulation(s)
                    project(s, "wout", lambda k: h[:, k])
                if s >= FIRST2:
                    last = (unit0[s + 1, FIRST_PHASE[subs[s + 1]]] if s + 1 < len(subs) else len(takes)) - 1
                    for k in range(KD):
                        pe.wait_ge(*taken(last - (KD - 1) + k))
                        ins = mm(pa[2][:, 0:T], ones[:], x[:, k], start=k == 0, stop=k == KD - 1)
                    ins.then_inc(s_mean_sums, 1)
                    squares_summed()



def tables():
    f = np.float32
    t = np.arange(T)
    out = {}
    inv = 1.0 / (10000.0 ** (np.arange(0, ROPE // 2, 2) / (ROPE // 2)))
    rope = np.zeros((QKD, 2, T))
    for half, pos in enumerate((t // 64, t % 64)):
        ang = (pos[None, :].astype(f) * inv[:, None].astype(f)).astype(f)
        for part in range(2):
            lo = NOPE + 16 * half + 8 * part
            rope[lo:lo + 8, 0], rope[lo:lo + 8, 1] = np.cos(ang), np.sin(ang)
    out["rope"] = rope.astype(f)
    rot = np.zeros((QKD, QKD), f)
    for half in range(2):
        for i in range(8):
            a = NOPE + 16 * half + i
            rot[a + 8, a], rot[a, a + 8] = -1.0, 1.0
    out["rot"] = rot
    out["ident"] = np.eye(P, dtype=f)
    ang = 2 * np.pi * (np.outer(t, t) % T) / T
    cs = np.concatenate([np.cos(ang), np.sin(ang)], 1).reshape(2, P, 512).transpose(1, 0, 2).reshape(P, 1024)
    ct = np.stack([np.cos(ang), -np.sin(ang)], 1).reshape(2, P, 512).transpose(1, 0, 2).reshape(P, 1024) / T
    out["dft"] = np.concatenate([cs, ct], 1).astype(f)[None]
    i = np.arange(P)
    S, U = i[:, None], i[None, :]
    lv = [(S // (2 * m) == U // (2 * m)) & (S % (2 * m) < m) & (U % (2 * m) >= m) for m in LEVELS]
    lv.append((S // 4 == U // 4) & (S <= U))
    out["masks"] = np.stack(lv, 1).astype(f)
    out["causal"] = (t[None, :] <= t[:, None]).reshape(TT, P, T).transpose(1, 0, 2).astype(f)
    pm = np.zeros((T, 4, T))
    for g, w in enumerate((2, 4, 8, 16)):
        for q in range(T):
            pm[max(0, q - w + 1):q + 1, g, q] = 1.0 / min(q + 1, w)
            pm[q, g, q] -= 1.0
    out["poolm"] = pm.reshape(TT, P, 4, T).transpose(1, 2, 0, 3).reshape(1, P, 2048).astype(f)
    dist = np.maximum(255 - np.arange(512), 0)
    exact = BUCKETS // 2
    large = exact + (np.log(np.maximum(dist, 1).astype(f) / f(exact)) / f(np.log(MAX_DIST / exact))
                     * f(BUCKETS - exact)).astype(np.int32)
    bucket = np.where(dist < exact, dist, np.minimum(large, BUCKETS - 1))
    out["onehot"] = (bucket[None, :] == np.arange(BUCKETS)[:, None]).astype(f).reshape(BUCKETS, 2, T)
    return {k: np.ascontiguousarray(v, dtype=f) for k, v in out.items()}



def feature_major(v):
    v = np.asarray(v)
    if v.ndim == 1:
        return v.reshape(-1, P).T
    return v.T.reshape(-1, P, v.shape[0]).transpose(1, 0, 2)


def blocks_of(w, per):
    k, n = w.shape
    return w.reshape(k // P, P, n // (P * per), per, P).transpose(2, 1, 3, 0, 4).reshape(n // (P * per), P, -1)


def rows_in(w):
    return w.reshape(-1, P, w.shape[1]).transpose(1, 0, 2).reshape(P, -1)


def gate_up(a, b):
    k, n = a.shape
    w = np.stack([a.reshape(k, n // P, P), b.reshape(k, n // P, P)], 2).reshape(k, 2 * n)
    return blocks_of(w, 4)


def layout(v):
    L = tables()
    L["x"] = feature_major(v["x"][0])
    L["ctx"] = feature_major(v["ctx"][0])
    L["cols"] = np.stack([feature_major(v["c"][0]), feature_major(v["c_ctx"]), feature_major(v["c_2"][0])], 1)
    ada = np.concatenate([v["ada_w"].reshape(DEPTH, D, 2, MODC).transpose(0, 2, 1, 3).reshape(4, D, MODC),
                          v["w_ada_2"].reshape(DEPTH, D, 3, MODC).transpose(0, 2, 1, 3).reshape(6, D, MODC)])
    L["ada"] = ada.reshape(10, KD, P, ADA_N, ADA_C).transpose(0, 3, 2, 1, 4).reshape(10 * ADA_N, P, KD, ADA_C)[FIRST_GATE:]
    L["ada_first"] = ada[0, :, :2 * D].reshape(KD, P, FIRST_N, 2, P).transpose(2, 1, 3, 0, 4).reshape(FIRST_N, P, 2 * D)
    L["ada_b"] = np.concatenate([v["ada_b"].reshape(4, 24, P), v["b_ada_2"].reshape(6, 24, P)]).transpose(2, 0, 1)
    gains = np.zeros((2, P), np.float32)
    gains[0, :QKD], gains[1, :QKD] = v["q_gain"][0], v["k_gain"][0]
    norm_g = np.stack([v["norm1_g"], v["norm2_g"]], 1)
    L["vec"] = np.concatenate([norm_g.reshape(-1, P), v["q_norm_g"].reshape(-1, P), v["kv_norm_g"].reshape(-1, P),
                               gains, v["conv_w"][0].reshape(-1, P), v["ln_g_2"].reshape(-1, P),
                               v["ln_b_2"].reshape(-1, P), v["pool_scale_2"].reshape(-1, P),
                               v["hgrn_lb_2"].reshape(-1, P), v["hgrn_norm_g_2"].reshape(-1, P)]).T
    L["poolw"] = v["pool_w_2"].reshape(DEPTH, 2, 2, 64, 64).transpose(2, 3, 0, 1, 4).reshape(P, DEPTH, 2, 64)
    rb = v["rel_bias_2"]
    L["relb"] = np.broadcast_to(rb[:, :, None], (BUCKETS, AH, P)).reshape(BUCKETS, 2, T)
    w = v["w_in"][0]
    at = QL + KVL
    L["w_in_a"] = blocks_of(w[:, 0:512], 4)
    L["w_in_b"] = np.concatenate([rows_in(w[:, 512:at]), rows_in(w[:, at:at + ROPE])], 1)[None]
    L["w_in_c"] = blocks_of(w[:, at + ROPE:], 4)
    L["w_uq"] = rows_in(v["w_uq"][0])[None]
    kv = v["w_ukv"][0].reshape(KVL, MLA_H, NOPE + VD)
    L["w_ukv"] = np.concatenate([rows_in(kv[:, :, :NOPE].reshape(KVL, -1)), rows_in(kv[:, :, NOPE:].reshape(KVL, -1))],
                                1)[None]
    L["w_o"] = blocks_of(v["w_o"][0], 4)
    L["w_f"] = blocks_of(v["w_fourier"][0], 4)
    w13 = [gate_up(v["ffn_w1"][i], v["ffn_w3"][i]) for i in range(DEPTH)]
    w2 = [blocks_of(v["ffn_w2"][i], 1) for i in range(DEPTH)]
    mproj, mlast, mtok, gates = [], [], [], []
    for l in range(DEPTH):
        for j in range(2):
            w = v["ffn_w_in_2"][l, j]
            w13.append(gate_up(w[:, :FF], w[:, FF:]))
            w2.append(blocks_of(v["ffn_w_out_2"][l, j], 1))
        w = v["mix_w_in_2"][l]
        a, q, k, val, qi, ki, wi, hq, hf, hi, hg, gt = np.split(
            w, np.cumsum([256, 256, 256, 256, 512, 64, 8, 512, 512, 512, 512]), axis=1)
        tiles = np.concatenate([hf, hq, qi, ki, ki, q, k, hg], 1)
        mproj.append(blocks_of(tiles[:, :20 * P], 4))
        mlast.append(np.concatenate([rows_in(tiles[:, 20 * P:]), rows_in(wi)], 1)[None])
        mtok.append(np.stack([rows_in(np.concatenate([a, val], 1)), rows_in(hi)]))
        gates.append(blocks_of(gt, 4))
    L["w13"], L["w2"] = np.stack(w13), np.stack(w2)
    L["mproj"], L["mlast"], L["mtok"], L["gates"] = map(np.stack, (mproj, mlast, mtok, gates))
    L["branch"] = np.stack([blocks_of(w, 4) for w in v["w_branch_2"]])
    L["wout"] = np.stack([blocks_of(w, 4) for w in v["w_out_2"]])
    return {k: np.ascontiguousarray(a) for k, a in L.items()}


def kernel(**inputs):
    import concourse.bacc as bacc
    from concourse.bass_utils import run_bass_kernel_spmd

    nc = bacc.Bacc("TRN2", target_bir_lowering=False, num_devices=1)
    laid = layout({k: np.asarray(a) for k, a in inputs.items()})
    I = {k: nc.dram_tensor(f"in_{k}", a.shape, mybir.dt.from_np(a.dtype), kind="ExternalInput").ap()
         for k, a in laid.items()}
    out = nc.dram_tensor("out", (P, KD, T), F32, kind="ExternalOutput").ap()
    build(nc, I, out)
    r = run_bass_kernel_spmd(nc, [{f"in_{k}": a for k, a in laid.items()}], core_ids=[0])
    y = r.results[0]["out"]
    return np.ascontiguousarray(y.transpose(1, 0, 2).reshape(D, T).T[None])
```
